# Optimizing a Trainium2 kernel written in Bass

```python
import math
import jax, jax.numpy as jnp
from jax import lax
import numpy as np

D_MODEL = 1024
BATCH = 1
SEQ = 1024
DEPTH = 1

D_MIX = D_MODEL
SSM_WIDTH = D_MIX // 2
SSM_GROUP = 16
SSM_GROUPS = SSM_WIDTH // SSM_GROUP
SSM_STATE = 64
MLA_HEADS = 4
QK_NOPE = 128
QK_ROPE = 64
QK_DIM = QK_NOPE + QK_ROPE
V_HEAD = 128
MLA_WIDTH = MLA_HEADS * V_HEAD
Q_LORA = 256
KV_LORA = 128
PLE_DIM = 256
ROPE_THETA = 10000.0
Q_BLOCK = 128
LN_EPS = 1e-5
RMS_EPS = 1e-6
DT_MIN = 1e-3
DT_MAX = 1e-1
MAX_POS_OFFSET = 4096
DEEPNORM_ALPHA = (2 * DEPTH) ** 0.25
DEEPNORM_BETA = (8 * DEPTH) ** -0.25

IN_SPLITS = (SSM_WIDTH, SSM_WIDTH, Q_LORA, KV_LORA, QK_ROPE, MLA_WIDTH)
D_IN = sum(IN_SPLITS)
IN_SPLIT_POINTS = tuple(int(v) for v in np.cumsum(IN_SPLITS)[:-1])


def layer_norm(x, g, b):
    xf = x.astype(jnp.float32)
    mu = jnp.mean(xf, axis=-1, keepdims=True)
    var = jnp.mean(jnp.square(xf - mu), axis=-1, keepdims=True)
    return ((xf - mu) * lax.rsqrt(var + LN_EPS)).astype(x.dtype) * g + b

def rms_norm(x, g):
    xf = x.astype(jnp.float32)
    return (xf * lax.rsqrt(jnp.mean(xf * xf, axis=-1, keepdims=True) + RMS_EPS)).astype(x.dtype) * g

def rope_tables(positions):
    inv_freq = 1.0 / (ROPE_THETA ** (jnp.arange(0, QK_ROPE, 2, dtype=jnp.float32) / QK_ROPE))
    ang = positions.astype(jnp.float32)[..., None] * inv_freq
    return jnp.cos(ang), jnp.sin(ang)

def rotary(x, cos, sin):
    xf = x.astype(jnp.float32)
    x1, x2 = jnp.split(xf, 2, axis=-1)
    return jnp.concatenate([x1 * cos - x2 * sin, x2 * cos + x1 * sin], axis=-1).astype(x.dtype)

def s5_branch(u, a_re, a_im, log_dt, b_re, b_im, c_re, c_im, d_skip, w_glu, b_glu):
    bsz, seqlen, _ = u.shape
    f32 = jnp.float32
    uf = u.astype(f32)
    ug = uf.reshape(bsz, seqlen, SSM_GROUPS, SSM_GROUP)
    a_re = a_re.astype(f32)
    a_im = a_im.astype(f32)
    dt = jnp.exp(log_dt.astype(f32))[:, None]
    mag = jnp.exp(dt * a_re)
    ab_re = mag * jnp.cos(dt * a_im)
    ab_im = mag * jnp.sin(dt * a_im)
    den = a_re * a_re + a_im * a_im
    nr = ab_re - 1.0
    k_re = (nr * a_re + ab_im * a_im) / den
    k_im = (ab_im * a_re - nr * a_im) / den
    bu_re = jnp.einsum('gpc,blgc->lbgp', b_re.astype(f32), ug)
    bu_im = jnp.einsum('gpc,blgc->lbgp', b_im.astype(f32), ug)
    x_re = k_re * bu_re - k_im * bu_im
    x_im = k_re * bu_im + k_im * bu_re
    a_seq_re = jnp.broadcast_to(ab_re, (seqlen, 1, SSM_GROUPS, SSM_STATE))
    a_seq_im = jnp.broadcast_to(ab_im, (seqlen, 1, SSM_GROUPS, SSM_STATE))

    def combine(left, right):
        al_re, al_im, bl_re, bl_im = left
        ar_re, ar_im, br_re, br_im = right
        return (al_re * ar_re - al_im * ar_im,
                al_re * ar_im + al_im * ar_re,
                ar_re * bl_re - ar_im * bl_im + br_re,
                ar_re * bl_im + ar_im * bl_re + br_im)

    _, _, h_re, h_im = lax.associative_scan(combine, (a_seq_re, a_seq_im, x_re, x_im), axis=0)
    y = (jnp.einsum('gcp,lbgp->blgc', c_re.astype(f32), h_re)
         - jnp.einsum('gcp,lbgp->blgc', c_im.astype(f32), h_im))
    y = y.reshape(bsz, seqlen, SSM_WIDTH) + d_skip.astype(f32) * uf
    y = jax.nn.gelu(y)
    y = y * jax.nn.sigmoid(y @ w_glu.astype(f32) + b_glu.astype(f32))
    return y.astype(u.dtype)

def mla_branch(cq, ckv, kr, cos, sin, q_norm_g, w_uq, kv_norm_g, w_ukv):
    bsz, seqlen, _ = cq.shape
    q = (rms_norm(cq, q_norm_g) @ w_uq).reshape(bsz, seqlen, MLA_HEADS, QK_DIM)
    q = jnp.concatenate([q[..., :QK_NOPE],
                         rotary(q[..., QK_NOPE:], cos[:, :, None, :], sin[:, :, None, :])], axis=-1)
    kv = (rms_norm(ckv, kv_norm_g) @ w_ukv).reshape(bsz, seqlen, MLA_HEADS, QK_NOPE + V_HEAD)
    k_nope, v = kv[..., :QK_NOPE], kv[..., QK_NOPE:]
    k_rope = rotary(kr, cos, sin)
    k = jnp.concatenate([k_nope, jnp.broadcast_to(k_rope[:, :, None, :],
                                                  (bsz, seqlen, MLA_HEADS, QK_ROPE))], axis=-1)
    scale = QK_DIM ** -0.5
    n_blocks = seqlen // Q_BLOCK
    q_blocks = q.reshape(bsz, n_blocks, Q_BLOCK, MLA_HEADS, QK_DIM).transpose(1, 0, 2, 3, 4)
    key_pos = jnp.arange(seqlen)

    def attend(args):
        qb, start = args
        s = jnp.einsum('bqhd,bkhd->bhqk', qb, k, preferred_element_type=jnp.float32) * scale
        q_pos = start + jnp.arange(Q_BLOCK)
        causal = key_pos[None, :] <= q_pos[:, None]
        s = jnp.where(causal, s, -jnp.inf)
        pr = jax.nn.softmax(s, axis=-1).astype(v.dtype)
        return jnp.einsum('bhqk,bkhd->bqhd', pr, v)

    out = lax.map(attend, (q_blocks, jnp.arange(n_blocks) * Q_BLOCK))
    return out.transpose(1, 0, 2, 3, 4).reshape(bsz, seqlen, MLA_WIDTH)

def first_inputs(seed: int = 0) -> dict:
    key = jax.random.key(seed)
    ks = jax.random.split(key, 26)
    f32 = jnp.float32
    nrm = lambda k, shape, s: jax.random.normal(k, shape, f32) * s
    x = jax.random.normal(ks[0], (BATCH, SEQ, D_MODEL), f32)
    p = jax.random.normal(ks[1], (DEPTH, BATCH, SEQ, PLE_DIM), f32)
    offsets = jax.random.randint(ks[2], (BATCH, 1), 0, MAX_POS_OFFSET, dtype=jnp.int32)
    positions = (jnp.arange(SEQ, dtype=jnp.int32)[None, :] + offsets).astype(jnp.int32)
    ln_emb_g = 1.0 + nrm(ks[3], (D_MODEL,), 0.05)
    ln_emb_b = nrm(ks[4], (D_MODEL,), 0.02)
    w_in = nrm(ks[5], (DEPTH, D_MODEL, D_IN), D_MODEL ** -0.5)
    a_re = -0.5 * jnp.exp(nrm(ks[6], (DEPTH, SSM_GROUPS, SSM_STATE), 0.05))
    a_im = math.pi * jnp.arange(SSM_STATE, dtype=f32) + nrm(ks[7], (DEPTH, SSM_GROUPS, SSM_STATE), 0.05)
    log_dt = jax.random.uniform(ks[8], (DEPTH, SSM_GROUPS), f32, math.log(DT_MIN), math.log(DT_MAX))
    b_re = nrm(ks[9], (DEPTH, SSM_GROUPS, SSM_STATE, SSM_GROUP), (2 * SSM_GROUP) ** -0.5)
    b_im = nrm(ks[10], (DEPTH, SSM_GROUPS, SSM_STATE, SSM_GROUP), (2 * SSM_GROUP) ** -0.5)
    c_re = nrm(ks[11], (DEPTH, SSM_GROUPS, SSM_GROUP, SSM_STATE), SSM_STATE ** -0.5)
    c_im = nrm(ks[12], (DEPTH, SSM_GROUPS, SSM_GROUP, SSM_STATE), SSM_STATE ** -0.5)
    d_skip = nrm(ks[13], (DEPTH, SSM_WIDTH), 1.0)
    w_glu = nrm(ks[14], (DEPTH, SSM_WIDTH, SSM_WIDTH), SSM_WIDTH ** -0.5)
    b_glu = nrm(ks[15], (DEPTH, SSM_WIDTH), 0.02)
    q_norm_g = 1.0 + nrm(ks[16], (DEPTH, Q_LORA), 0.05)
    w_uq = nrm(ks[17], (DEPTH, Q_LORA, MLA_HEADS * QK_DIM), Q_LORA ** -0.5)
    kv_norm_g = 1.0 + nrm(ks[18], (DEPTH, KV_LORA), 0.05)
    w_ukv = nrm(ks[19], (DEPTH, KV_LORA, MLA_HEADS * (QK_NOPE + V_HEAD)), KV_LORA ** -0.5)
    w_out = nrm(ks[20], (DEPTH, D_MIX, D_MODEL), D_MIX ** -0.5 * DEEPNORM_BETA)
    w_pg = nrm(ks[21], (DEPTH, D_MODEL, D_MODEL), D_MODEL ** -0.5)
    w_pp = nrm(ks[22], (DEPTH, PLE_DIM, D_MODEL), PLE_DIM ** -0.5 * DEEPNORM_BETA)
    ln_g = 1.0 + nrm(ks[23], (DEPTH, D_MODEL), 0.05)
    ln_b = nrm(ks[24], (DEPTH, D_MODEL), 0.02)
    return {"x": x, "p": p, "positions": positions, "ln_emb_g": ln_emb_g, "ln_emb_b": ln_emb_b,
            "w_in": w_in, "a_re": a_re, "a_im": a_im, "log_dt": log_dt,
            "b_re": b_re, "b_im": b_im, "c_re": c_re, "c_im": c_im, "d_skip": d_skip,
            "w_glu": w_glu, "b_glu": b_glu, "q_norm_g": q_norm_g, "w_uq": w_uq,
            "kv_norm_g": kv_norm_g, "w_ukv": w_ukv, "w_out": w_out, "w_pg": w_pg,
            "w_pp": w_pp, "ln_g": ln_g, "ln_b": ln_b}

def first_block(x, p, positions, ln_emb_g, ln_emb_b, w_in, a_re, a_im, log_dt,
              b_re, b_im, c_re, c_im, d_skip, w_glu, b_glu, q_norm_g, w_uq,
              kv_norm_g, w_ukv, w_out, w_pg, w_pp, ln_g, ln_b):
    x = layer_norm(x, ln_emb_g, ln_emb_b)
    cos, sin = rope_tables(positions)
    for i in range(DEPTH):
        z = x @ w_in[i]
        xs, gs, cq, ckv, kr, gm = jnp.split(z, IN_SPLIT_POINTS, axis=-1)
        ys = s5_branch(xs, a_re[i], a_im[i], log_dt[i], b_re[i], b_im[i], c_re[i], c_im[i],
                       d_skip[i], w_glu[i], b_glu[i]) * jax.nn.silu(gs)
        ym = mla_branch(cq, ckv, kr, cos, sin, q_norm_g[i], w_uq[i], kv_norm_g[i],
                        w_ukv[i]) * jax.nn.silu(gm)
        mix = jnp.concatenate([ys, ym], axis=-1) @ w_out[i]
        u = DEEPNORM_ALPHA * x + mix
        ple = jax.nn.sigmoid(u @ w_pg[i]) * (p[i] @ w_pp[i])
        x = layer_norm(u + ple, ln_g[i], ln_b[i])
    return x


GRID_W = 64
HEAD_DIM = 64
N_HEADS_DIL = 8
N_HEADS_NA = 8
WIDTH_DIL = N_HEADS_DIL * HEAD_DIM
WIDTH_NA = N_HEADS_NA * HEAD_DIM
DIL_PATTERNS = ((128, 1), (512, 4), (2048, 16))
QUERY_BLOCK = 64
NA_ROWS_MAX = 8
NA_COLS = 16
T5_BUCKETS = 32
T5_MAX_DISTANCE = 1024
D_FF = 2816
CONV_WIDTH = 3
IN_SPLITS_2 = (WIDTH_DIL, WIDTH_DIL, WIDTH_DIL, WIDTH_NA, WIDTH_NA, WIDTH_NA, D_MODEL, D_MODEL)
IN_COLS = sum(IN_SPLITS_2)


def rmsnorm(x, g):
    x32 = x.astype(jnp.float32)
    y = x32 * lax.rsqrt(jnp.mean(x32 * x32, axis=-1, keepdims=True) + RMS_EPS)
    return (y * g.astype(jnp.float32)).astype(x.dtype)

def t5_bucket(rel):
    n = T5_BUCKETS // 2
    max_exact = n // 2
    sign_part = jnp.where(rel > 0, n, 0)
    a = jnp.abs(rel)
    af = jnp.maximum(a, 1).astype(jnp.float32)
    large = max_exact + (jnp.log(af / max_exact) / math.log(T5_MAX_DISTANCE / max_exact)
                         * (n - max_exact)).astype(jnp.int32)
    large = jnp.minimum(large, n - 1)
    return sign_part + jnp.where(a < max_exact, a, large)

def dilated_window_attention(q, k, v, rel_bias, window, dilation):
    B, S, H, Dh = q.shape
    L = S // dilation
    R = window // (2 * dilation)
    nb = -(-L // QUERY_BLOCK)
    Lp = nb * QUERY_BLOCK
    KB = QUERY_BLOCK + 2 * R

    def to_res(t):
        return t.reshape(B, L, dilation, H, Dh).transpose(0, 2, 1, 3, 4)

    qr, kr, vr = to_res(q), to_res(k), to_res(v)
    qb = jnp.pad(qr, ((0, 0), (0, 0), (0, Lp - L), (0, 0), (0, 0))).reshape(B, dilation, nb, QUERY_BLOCK, H, Dh)
    pad_kv = ((0, 0), (0, 0), (R, Lp - L + R), (0, 0), (0, 0))
    key_idx = jnp.arange(nb)[:, None] * QUERY_BLOCK + jnp.arange(KB)[None, :]
    kb = jnp.pad(kr, pad_kv)[:, :, key_idx]
    vb = jnp.pad(vr, pad_kv)[:, :, key_idx]

    delta = jnp.arange(KB)[None, :] - jnp.arange(QUERY_BLOCK)[:, None] - R
    key_pos = key_idx - R
    mask = ((key_pos >= 0) & (key_pos < L))[:, None, :] & (jnp.abs(delta) <= R)[None]
    bias = rel_bias[t5_bucket(delta * dilation)].astype(jnp.float32).transpose(2, 0, 1)

    scale = HEAD_DIM ** -0.5
    s = jnp.einsum('bgnqhd,bgnkhd->bghnqk', qb, kb).astype(jnp.float32) * scale + bias[:, None]
    s = jnp.where(mask, s, -jnp.inf)
    m = jnp.max(s, axis=-1, keepdims=True)
    p = jnp.exp(s - m)
    l = jnp.sum(p, axis=-1, keepdims=True)
    o = jnp.einsum('bghnqk,bgnkhd->bgnqhd', (p / l).astype(v.dtype), vb)
    lse = (m + jnp.log(l))[..., 0]

    o = o.reshape(B, dilation, Lp, H, Dh)[:, :, :L].transpose(0, 2, 1, 3, 4).reshape(B, S, H, Dh)
    lse = lse.transpose(0, 1, 3, 4, 2).reshape(B, dilation, Lp, H)[:, :, :L]
    lse = lse.transpose(0, 2, 1, 3).reshape(B, S, H)
    return o, lse

def mixture_of_dilations(q, k, v, rel_bias):
    outs, lses = [], []
    for window, dilation in DIL_PATTERNS:
        o, lse = dilated_window_attention(q, k, v, rel_bias, window, dilation)
        outs.append(o)
        lses.append(lse)
    w = jax.nn.softmax(jnp.stack(lses, axis=0), axis=0)
    return jnp.einsum('gbsh,gbshd->bshd', w.astype(q.dtype), jnp.stack(outs, axis=0))

def neighbourhood_attention_2d(q, k, v, rpb):
    B, S, H, Dh = q.shape
    rows = S // GRID_W
    kh = min(NA_ROWS_MAX, rows)
    q5 = q.reshape(B, rows, GRID_W, H, Dh)
    k5 = k.reshape(B, rows, GRID_W, H, Dh)
    v5 = v.reshape(B, rows, GRID_W, H, Dh)

    r = jnp.arange(rows)
    row_start = jnp.clip(r - kh // 2, 0, rows - kh)
    row_idx = row_start[:, None] + jnp.arange(kh)[None, :]
    kr = k5[:, row_idx]
    vr = v5[:, row_idx]

    cq = jnp.arange(GRID_W)
    col_start = jnp.clip(cq - NA_COLS // 2, 0, GRID_W - NA_COLS)
    col_mask = (cq[None, :] >= col_start[:, None]) & (cq[None, :] < col_start[:, None] + NA_COLS)

    dr = row_idx - r[:, None]
    dc = jnp.clip(cq[None, :] - cq[:, None], -(NA_COLS - 1), NA_COLS - 1)
    bias = rpb.astype(jnp.float32)[:, (dr + NA_ROWS_MAX - 1)[:, :, None, None], (dc + NA_COLS - 1)[None, None]]
    bias = bias.transpose(0, 1, 3, 2, 4)

    scale = HEAD_DIM ** -0.5
    s = jnp.einsum('brqhd,brakhd->bhrqak', q5, kr).astype(jnp.float32) * scale + bias[None]
    s = jnp.where(col_mask[:, None, :], s, -jnp.inf)
    p = jax.nn.softmax(s, axis=(-2, -1))
    o = jnp.einsum('bhrqak,brakhd->brqhd', p.astype(v.dtype), vr)
    return o.reshape(B, S, H, Dh)

def depthwise_conv_seq(u, w, b):
    C = u.shape[-1]
    pad = CONV_WIDTH // 2
    y = lax.conv_general_dilated(u, w.astype(u.dtype)[:, None, :], window_strides=(1,),
                                 padding=((pad, pad),), dimension_numbers=('NWC', 'WIO', 'NWC'),
                                 feature_group_count=C)
    return y + b.astype(u.dtype)

def second_inputs(seed: int = 0) -> dict:
    key = jax.random.key(seed)
    ks = jax.random.split(key, 20)
    f32 = jnp.float32
    nrm = lambda k, shape, s: (jax.random.normal(k, shape, f32) * s)
    return {
        "x": nrm(ks[0], (BATCH, SEQ, D_MODEL), 1.0),
        "c": nrm(ks[1], (BATCH, D_MODEL), 1.0),
        "w_ada": nrm(ks[2], (DEPTH, D_MODEL, 6 * D_MODEL), D_MODEL ** -0.5),
        "b_ada": nrm(ks[3], (DEPTH, 6 * D_MODEL), 0.02),
        "g_mix": 1.0 + nrm(ks[4], (DEPTH, D_MODEL), 0.02),
        "w_in": nrm(ks[5], (DEPTH, D_MODEL, IN_COLS), D_MODEL ** -0.5),
        "rel_bias": nrm(ks[6], (T5_BUCKETS, N_HEADS_DIL), 0.5),
        "na_rpb": nrm(ks[7], (DEPTH, N_HEADS_NA, 2 * NA_ROWS_MAX - 1, 2 * NA_COLS - 1), 0.5),
        "w_branch_dil": nrm(ks[8], (DEPTH, WIDTH_DIL, D_MODEL), WIDTH_DIL ** -0.5),
        "w_branch_na": nrm(ks[9], (DEPTH, WIDTH_NA, D_MODEL), WIDTH_NA ** -0.5),
        "w_out": nrm(ks[10], (DEPTH, D_MODEL, D_MODEL), D_MODEL ** -0.5),
        "g_ffn": 1.0 + nrm(ks[11], (DEPTH, D_MODEL), 0.02),
        "w_up": nrm(ks[12], (DEPTH, D_MODEL, 2 * D_FF), D_MODEL ** -0.5),
        "conv_w": nrm(ks[13], (DEPTH, CONV_WIDTH, 2 * D_FF), CONV_WIDTH ** -0.5),
        "conv_b": nrm(ks[14], (DEPTH, 2 * D_FF), 0.01),
        "w_down": nrm(ks[15], (DEPTH, D_FF, D_MODEL), D_FF ** -0.5),
        "g_final": 1.0 + nrm(ks[16], (D_MODEL,), 0.02),
    }

def second_block(x, c, w_ada, b_ada, g_mix, w_in, rel_bias, na_rpb, w_branch_dil, w_branch_na,
              w_out, g_ffn, w_up, conv_w, conv_b, w_down, g_final):
    B, S, D = x.shape
    split_at = list(np.cumsum(IN_SPLITS_2)[:-1])
    for i in range(DEPTH):
        ada = jax.nn.silu(c) @ w_ada[i] + b_ada[i]
        shift1, scale1, gate1, shift2, scale2, gate2 = [t[:, None, :] for t in jnp.split(ada, 6, axis=-1)]

        h = rmsnorm(x, g_mix[i]) * (1 + scale1) + shift1
        proj = h @ w_in[i]
        qa, ka, va, qb, kb, vb, ga, gb = jnp.split(proj, split_at, axis=-1)
        heads = lambda t, n: t.reshape(B, S, n, HEAD_DIM)
        oa = mixture_of_dilations(heads(qa, N_HEADS_DIL), heads(ka, N_HEADS_DIL), heads(va, N_HEADS_DIL), rel_bias)
        ob = neighbourhood_attention_2d(heads(qb, N_HEADS_NA), heads(kb, N_HEADS_NA), heads(vb, N_HEADS_NA), na_rpb[i])
        ya = oa.reshape(B, S, WIDTH_DIL) @ w_branch_dil[i]
        yb = ob.reshape(B, S, WIDTH_NA) @ w_branch_na[i]
        merged = jax.nn.sigmoid(ga) * ya + jax.nn.sigmoid(gb) * yb
        x = x + gate1 * (merged @ w_out[i])

        h2 = rmsnorm(x, g_ffn[i]) * (1 + scale2) + shift2
        u = depthwise_conv_seq(h2 @ w_up[i], conv_w[i], conv_b[i])
        u_val, u_gate = jnp.split(u, 2, axis=-1)
        x = x + gate2 * ((jax.nn.gelu(u_gate, approximate=True) * u_val) @ w_down[i])
    return rmsnorm(x, g_final)


def setup_inputs(seed=0):
    out = dict(first_inputs(seed))
    for name, value in second_inputs(seed + 1).items():
        if name != "x":
            out[name + "_2"] = value
    return out


def reference(
    x, p, positions, ln_emb_g, ln_emb_b, w_in, a_re, a_im, log_dt, b_re, b_im, c_re, c_im,
    d_skip, w_glu, b_glu, q_norm_g, w_uq, kv_norm_g, w_ukv, w_out, w_pg, w_pp, ln_g, ln_b, c_2,
    w_ada_2, b_ada_2, g_mix_2, w_in_2, rel_bias_2, na_rpb_2, w_branch_dil_2, w_branch_na_2,
    w_out_2, g_ffn_2, w_up_2, conv_w_2, conv_b_2, w_down_2, g_final_2,
):
    x = first_block(
        x, p, positions, ln_emb_g, ln_emb_b, w_in, a_re, a_im, log_dt, b_re, b_im, c_re, c_im,
        d_skip, w_glu, b_glu, q_norm_g, w_uq, kv_norm_g, w_ukv, w_out, w_pg, w_pp, ln_g, ln_b,
    )
    return second_block(
        x, c_2, w_ada_2, b_ada_2, g_mix_2, w_in_2, rel_bias_2, na_rpb_2, w_branch_dil_2,
        w_branch_na_2, w_out_2, g_ffn_2, w_up_2, conv_w_2, conv_b_2, w_down_2, g_final_2,
    )


_drawn_inputs = setup_inputs


def setup_inputs(seed=0):
    import zlib

    import numpy as np

    out = dict(_drawn_inputs(seed))
    spreads = {}
    factors = {'a_re': 64.0,
     'a_im': 64.0,
     'log_dt': 64.0,
     'b_re': 64.0,
     'b_im': 64.0,
     'c_re': 64.0,
     'c_im': 64.0,
     'b_glu': 8.0,
     'q_norm_g': 8.0,
     'kv_norm_g': 8.0,
     'g_mix_2': 8.0,
     'g_ffn_2': 3.758,
     'conv_b_2': 8.0,
     'g_final_2': 2.704}
    for name, (base, spread) in spreads.items():
        noise = np.random.default_rng([zlib.crc32(name.encode()), seed]).standard_normal(out[name].shape)
        drawn = base * np.exp(spread * noise) if base else spread * noise
        out[name] = __import__('jax').numpy.asarray(drawn.astype(out[name].dtype))
    for name, factor in factors.items():
        out[name] = (out[name] * factor).astype(out[name].dtype)
    return out
```

```python
import math
from contextlib import ExitStack

import numpy as np

import concourse.bass as bass
from concourse import mybir

F32 = mybir.dt.float32
I32 = mybir.dt.int32
ALU = mybir.AluOpType
ACT = mybir.ActivationFunctionType

P = 128
SEQ = 1024
D = 1024
FT = D // P
BANK = 512
PAGE = 1024
RING = 4
LN_EPS, RMS_EPS = 1e-5, 1e-6
ALPHA = 2.0 ** 0.25
MASKED = -1e30

GROUPS, GC, STATE = 32, 16, 64
PAIRS = GROUPS // 2
STEP = P // GC
CHUNKS = SEQ // STEP
MLA_HEADS = 4
MLA_SCALE = (128 + 64) ** -0.5
HEADS2, HD = 8, 64
N_UP = 22

_TWO_PI = 2 * math.pi
TP1 = float(np.float32(round(_TWO_PI * 2 ** 9) / 2 ** 9))
TP2 = float(np.float32(round((_TWO_PI - TP1) * 2 ** 22) / 2 ** 22))
TP3 = float(np.float32(_TWO_PI - TP1 - TP2))
ROUND = float(1.5 * 2 ** 23)
PI_IN = 3.1415925

VEC = {}
_at = 0
for _name, _n in (("ln_emb_g", 8), ("ln_emb_b", 8), ("b_glu", 4), ("q_norm_g", 2), ("kv_norm_g", 1),
                  ("ln_g", 8), ("ln_b", 8), ("c", 8), ("b_ada", 48), ("g_mix", 8), ("g_ffn", 8),
                  ("conv_w", 3 * 2 * N_UP), ("conv_b", 2 * N_UP), ("g_final", 8)):
    VEC[_name] = (_at, _n)
    _at += _n
N_VEC = _at


def program(nc, t, out, debug=None):
    with ExitStack() as ctx:
        sems = {}

        def S(name):
            if name not in sems:
                sems[name] = ctx.enter_context(nc.semaphore(name))
            return sems[name]

        arena = ctx.enter_context(nc.sbuf_tensor("arena", [P, 50 * PAGE], F32))
        ps = ctx.enter_context(nc.psum_tensor("ps", [P, 8, BANK], F32))

        def sb(name, cols, dt=F32):
            return ctx.enter_context(nc.sbuf_tensor(f"sb_{name}", [P, cols], dt))

        def page(a, n=1, off=0):
            return arena[:, a * PAGE + off:(a + n) * PAGE + off]

        def pages(a, n):
            return page(a, n).rearrange("p (k t) -> p k t", k=n)

        def two(b):
            return ps[:, b:b + 2, :].rearrange("p a b -> p (a b)")

        vec = sb("vec", N_VEC)
        ident = sb("ident", P)
        ones = sb("ones", P)
        rope_c = sb("rope_c", 2)
        eps = sb("eps", 2)
        csilu = sb("csilu", 8)
        ada = sb("ada", 48)
        stat = sb("stat", 16)
        small = sb("small", 24 * PAIRS)
        ptab = sb("ptab", 2 * PAIRS * 9)
        dsk = sb("dsk", GROUPS)
        ones_q = sb("ones_q", P)
        ones_kv = sb("ones_kv", P)
        ada_raw = sb("ada_raw", 48)

        def V(name, k):
            a, _ = VEC[name]
            return vec[:, a + k:a + k + 1]

        def VV(name):
            a, n = VEC[name]
            return vec[:, a:a + n]

        ring = pages(0, RING)
        XN = pages(4, FT)
        XS = pages(12, 4)
        SS = page(12, 4).rearrange("p (i q n) -> p i q n", i=2, q=PAIRS)
        YF = pages(12, 4)
        GS = pages(16, 4)
        WB = page(20, 4).rearrange("p (i q n) -> p i q n", i=2, q=PAIRS)
        CQ = pages(20, 2)
        CKV = page(22)
        KR = page(23)
        GSB = page(24, 4).rearrange("p (g n) -> p g n", g=GROUPS)
        GM = pages(24, 4)
        UU = page(28, 4).rearrange("p (g n) -> p g n", g=GROUPS)
        TMPA = page(28, 2)
        TMPB = page(30, 2)
        PW = page(32, 4).rearrange("p (q i n) -> p q i n", q=PAIRS, i=2)
        TM = page(36, 4).rearrange("p (g n) -> p g n", g=GROUPS)
        CP = arena[:, 40 * PAGE:40 * PAGE + 2 * PAIRS * 144].rearrange("p (i q n) -> p i q n", i=2, q=PAIRS)
        _e0 = 40 * PAGE + 2 * PAIRS * 144
        EE = arena[:, _e0:_e0 + 2 * PAIRS * CHUNKS].rearrange("p (i q n) -> p i q n", i=2, q=PAIRS)
        _bc = 48 * PAGE + 512
        BC = arena[:, _bc:_bc + 4 * 256].rearrange("p (i q c) -> p i q c", i=4, q=PAIRS)
        KB = arena[:, _bc + 1024:_bc + 1024 + 512].rearrange("p (i q c) -> p i q c", i=2, q=PAIRS)
        QN, QR, KN = pages(28, 4), pages(32, 4), pages(36, 4)
        VT = pages(40, 4).rearrange("p k (a d) -> p (k a) d", a=2)
        KROT, CM = page(44), page(45)
        COS, SIN = page(48), page(49)
        OBUF = [page(12 + i).rearrange("p (k d) -> p k d", k=8) for i in range(2)]
        FINAL = pages(42, FT)
        PP, PT_IN = pages(28, FT), pages(36, 2)
        X2 = pages(42, FT)

        def sm(x):
            return small[:, x * PAIRS:(x + 1) * PAIRS]

        x_dram = nc.dram_tensor("ssm_in_by_feature", (512, SEQ), F32, kind="Internal").ap()
        y_dram = nc.dram_tensor("ssm_out_by_feature", (512, SEQ), F32, kind="Internal").ap()

        Q2, K2 = pages(12, 8), pages(20, 4)
        V2 = page(24, 4).rearrange("p (k d) -> p k d", k=8)
        OAT = pages(28, 4)
        ONT = [page(12 + 2 * k) for k in range(4)]
        TB = [arena[:, 37 * PAGE:37 * PAGE + 1920], arena[:, 39 * PAGE:39 * PAGE + 1920]]
        NB = [arena[:, 37 * PAGE:37 * PAGE + 1536], arena[:, 37 * PAGE + 1536:40 * PAGE]]
        COLM = arena[:, 40 * PAGE:40 * PAGE + 64]
        ROWM = arena[:, 40 * PAGE + 64:40 * PAGE + 704]
        MRG, GT = pages(20, FT), pages(32, 4)
        ACTV, UPB = pages(12, N_UP), pages(34, 4)
        TEMPS_4 = (page(34), page(35), page(36))
        relb, gains = sb("relb", 8), sb("gains", 16)
        dist_dram = nc.dram_tensor("bias_by_distance", (HEADS2, 2048), F32, kind="Internal").ap()
        conv = vec[:, VEC["conv_w"][0]:VEC["conv_w"][0] + 8 * N_UP]

        def pg(view, m):
            return view[:, m, :] if isinstance(m, int) else \
                view[:, bass.ds(m, 1), :].rearrange("p k t -> p (k t)")

        def one(view, m):
            return view[:, m:m + 1] if isinstance(m, int) else view[:, bass.ds(m, 1)]

        block = ctx.enter_context(nc.Block())

        def turned_at(k):
            return slice((k % 2) * BANK + k // 2 * P, (k % 2) * BANK + k // 2 * P + P)

        def odd_copies(items, j):
            return sum(it[2] > P for it in items[:j + 1])

        LAG = 1

        def steps_of(items, per_turn, turns):
            out_, left = [], list(range(len(turns)))
            for i in range(len(items)):
                out_.append(i)
                if left and i == (left[0] + 1) * per_turn + LAG + 2:
                    out_.append(str(left.pop(0)))
            return out_ + [None] * (LAG + 1) + [str(x) for x in left]

        def attention_pe(pe, A, bufs, items, per_turn, turns):
            SBUF, PTB = bufs
            n, step, used = len(items), 0, 0
            for what in steps_of(items, per_turn, turns):
                if what is not None:
                    if used >= 2:
                        pe.wait_ge(S(f"{A}_scores_read"), used - 1)
                    pair = two(2 * (used % 2))
                    used += 1
                if isinstance(what, str):
                    x = int(what)
                    pe.wait_ge(S(f"{A}_out_read"), (x + 1) * per_turn)
                    for k in range(8):
                        mm = pe.transpose(pair[:, k * P:(k + 1) * P], turns[x][0][:, k, :], ident[:])
                    mm.then_inc(S(f"{A}_scores"), 1)
                    continue
                i = step
                step += 1
                if i < n:
                    for c0, c1, lhsT, rhs, st, sp_ in items[i][0]:
                        mm = pe.matmul(pair[:, c0:c1], lhsT, rhs, start=st, stop=sp_)
                    mm.then_inc(S(f"{A}_scores"), 1)
                j = i - LAG
                if 0 <= j < n:
                    w = items[j][2]
                    pe.wait_ge(S(f"{A}_exp"), j + 1)
                    if j >= 1:
                        pe.wait_ge(S(f"{A}_pt_dve"), j)
                        if odd_copies(items, j - 1):
                            pe.wait_ge(S(f"{A}_pt_act"), odd_copies(items, j - 1))
                    for k in range(w // P):
                        mm = pe.transpose(two(4)[:, turned_at(k)],
                                          SBUF[j % NSB][:, k * P:(k + 1) * P], ident[:])
                    mm.then_inc(S(f"{A}_turned"), 1)
                j = i - LAG - 1
                if 0 <= j < n:
                    w, values, d = items[j][2:5]
                    pe.wait_ge(S(f"{A}_pt_dve"), j + 1)
                    if odd_copies(items, j):
                        pe.wait_ge(S(f"{A}_pt_act"), odd_copies(items, j))
                    if j >= 2:
                        pe.wait_ge(S(f"{A}_out_read"), j - 1)
                    for k in range(w // P):
                        mm = pe.matmul(ps[:, 6 + j % 2, 0:d], PTB[j % 2][:, turned_at(k)], values(k),
                                       start=k == 0, stop=k == w // P - 1)
                    mm.then_inc(S(f"{A}_out"), 1)

        def attention_dve(dve, A, bufs, items, per_turn, turns, scale, before):
            SBUF, PTB = bufs
            n, step, used = len(items), 0, 0
            for what in steps_of(items, per_turn, turns):
                if what is not None:
                    pair = two(2 * (used % 2))
                    used += 1
                if isinstance(what, str):
                    _, dst, times = turns[int(what)]
                    dve.wait_ge(S(f"{A}_scores"), used)
                    if times is None:
                        dve.tensor_copy(dst, pair).then_inc(S(f"{A}_scores_read"), 1)
                    else:
                        dve.tensor_tensor(dst, pair, times, ALU.mult).then_inc(S(f"{A}_scores_read"), 1)
                    continue
                i = step
                step += 1
                if i < n:
                    bias, w = items[i][1:3]
                    before(i)
                    dve.wait_ge(S(f"{A}_scores"), used)
                    if i >= NSB:
                        dve.wait_ge(S(f"{A}_turned"), i - NSB + 1)
                    dve.tensor_tensor_reduce(SBUF[i % NSB][:, 0:w], pair[:, 0:w], bias, 1.0,
                                             -3e38, ALU.add, ALU.max, stat[:, i % 4:i % 4 + 1])\
                        .then_inc(S(f"{A}_scores_read"), 1)
                    dve.wait_ge(S(f"{A}_scores_read"), used)
                    dve.tensor_scalar(stat[:, 4 + i % 4:5 + i % 4], stat[:, i % 4:i % 4 + 1], -scale, None,
                                      ALU.mult).then_inc(S(f"{A}_negmax"), 1)
                j = i - LAG
                if 0 <= j < n:
                    h = (items[j][2] // P + 1) // 2 * P
                    dve.wait_ge(S(f"{A}_exp"), j + 1)
                    dve.reciprocal(stat[:, 12 + j % 4:13 + j % 4], stat[:, 8 + j % 4:9 + j % 4])\
                        .then_inc(S(f"{A}_recip"), 1)
                    dve.wait_ge(S(f"{A}_turned"), j + 1)
                    if j >= 2:
                        dve.wait_ge(S(f"{A}_out"), j - 1)
                    dve.tensor_copy(PTB[j % 2][:, 0:h], two(4)[:, 0:h]).then_inc(S(f"{A}_pt_dve"), 1)
                j = i - LAG - 1
                if 0 <= j < n:
                    d, o = items[j][4:6]
                    dve.wait_ge(S(f"{A}_out"), j + 1)
                    dve.wait_ge(S(f"{A}_recip"), j + 1)
                    dve.tensor_scalar(o, ps[:, 6 + j % 2, 0:d], stat[:, 12 + j % 4:13 + j % 4], None,
                                      ALU.mult).then_inc(S(f"{A}_out_read"), 1)

        def attention_act(act, A, bufs, items, scale):
            SBUF, PTB = bufs
            n = len(items)
            for i in range(n + LAG):
                if i < n:
                    w = items[i][2]
                    act.wait_ge(S(f"{A}_negmax"), i + 1)
                    if i >= 4:
                        act.wait_ge(S(f"{A}_recip"), i - 3)
                    act.activation(SBUF[i % NSB][:, 0:w], SBUF[i % NSB][:, 0:w], ACT.Exp,
                                   bias=stat[:, 4 + i % 4:5 + i % 4], scale=scale,
                                   accum_out=stat[:, 8 + i % 4:9 + i % 4]).then_inc(S(f"{A}_exp"), 1)
                j = i - LAG
                if 0 <= j < n:
                    w = items[j][2]
                    if w > P:
                        h = w // P // 2 * P
                        act.wait_ge(S(f"{A}_turned"), j + 1)
                        if j >= 2:
                            act.wait_ge(S(f"{A}_out"), j - 1)
                        act.activation(PTB[j % 2][:, BANK:BANK + h], two(4)[:, BANK:BANK + h], ACT.Copy)\
                            .then_inc(S(f"{A}_pt_act"), 1)

        def scores_used(items, per_turn, turns, i):
            return [w for w in steps_of(items, per_turn, turns) if w is not None].index(i) + 1

        NSB = 3
        BUFS_1 = ([page(20), page(21), page(22)], [page(47), page(23)])
        BUFS_2 = ([page(32), page(33), page(34)], [page(35), page(36)])

        def mla_items():
            items = []
            for h in range(MLA_HEADS):
                for qb in range(8):
                    w = (qb + 1) * P
                    q = slice(qb * P, (qb + 1) * P)
                    sc = []
                    for c0 in range(0, w, BANK):
                        c1 = min(w, c0 + BANK)
                        sc.append((c0, c1, QN[:, h, q], KN[:, h, c0:c1], True, False))
                        sc.append((c0, c1, QR[:, h, q], KROT[:, c0:c1], False, True))
                    items.append((sc, CM[:, SEQ - w:SEQ], w,
                                  lambda k, h=h: VT[:, k, h * P:(h + 1) * P], P,
                                  OBUF[h % 2][:, qb, :]))
            turns = [(OBUF[h % 2], GM[:, h, :], GM[:, h, :]) for h in range(MLA_HEADS)]
            return items, 8, turns

        def out_pages(second_out):
            return [p_.rearrange("p (k d) -> p k d", k=8) for p_ in (page(41), second_out)]

        def dil_items():
            obuf = out_pages(page(12))
            items = []
            for h in range(HEADS2):
                for qb in range(8):
                    sc = [(c, c + BANK, Q2[:, h, qb * P:(qb + 1) * P], K2[:, h // 2, c:c + BANK], True, True)
                          for c in (0, BANK)]
                    items.append((sc, TB[h % 2][:, P * qb:P * qb + SEQ][:, ::-1], SEQ,
                                  lambda k, h=h: V2[:, k, h * HD:(h + 1) * HD], HD,
                                  obuf[h // 2 % 2][:, qb, (h % 2) * HD:(h % 2) * HD + HD]))
            return items, 16, [(obuf[x % 2], OAT[:, x, :], None) for x in range(4)]

        def na_items():
            obuf = out_pages(page(13))
            items = []
            for h in range(HEADS2):
                for qb in range(8):
                    row0 = min(max(2 * qb - 4, 0), 8)
                    inner = 2 <= qb <= 5
                    w = 640 if inner else BANK
                    k0 = row0 * 64
                    sc = [(c, min(c + BANK, w), Q2[:, h, qb * P:(qb + 1) * P],
                           K2[:, h // 2, k0 + c:k0 + min(c + BANK, w)], True, True) for c in range(0, w, BANK)]
                    a = 2 * qb * 64 - k0
                    bias = NB[h % 2][:, 896:1536][:, ::-1] if inner else NB[h % 2][:, a:a + BANK][:, ::-1]
                    items.append((sc, bias, w,
                                  lambda k, h=h, k0=k0: V2[:, k0 // P + k, h * HD:(h + 1) * HD], HD,
                                  obuf[h // 2 % 2][:, qb, (h % 2) * HD:(h % 2) * HD + HD]))
            return items, 16, [(obuf[x % 2], ONT[x], None) for x in range(4)]

        NORMS = {"ln_emb": 8, "kv_norm": 1, "q_norm": 2, "ln_1": 8, "rms_mix": 8, "rms_ffn": 8, "final": 8}

        def tiles_to(N, k):
            names = list(NORMS)
            return sum(NORMS[x] for x in names[:names.index(N)]) + k

        def norms_to(N):
            return list(NORMS).index(N) + 1

        def centred_to(N, k):
            return (FT if N == "ln_1" else 0) + k

        def norm_pe(pe, N, kts, src, ones_, centered, T):
            if centered:
                for k in range(kts):
                    for nt in range(2):
                        mm = pe.matmul(ps[:, nt, :], ones_, src(k)[:, nt * BANK:(nt + 1) * BANK],
                                       start=k == 0, stop=k == kts - 1)
                mm.then_inc(S("norm_mean"), 1)
            for k in range(kts):
                pe.wait_ge(S("norm_square"), tiles_to(N, k + 1))
                for nt in range(2):
                    mm = pe.matmul(ps[:, 2 + nt, :], ones_, T[k % 2][:, nt * BANK:(nt + 1) * BANK],
                                   start=k == 0, stop=k == kts - 1)
                mm.then_inc(S("norm_square_used"), 1)

        def norm_act(act, N, kts, src, dst, gain, bias, epscol, centered, T):
            for k in range(kts):
                if centered:
                    act.wait_ge(S("norm_centred"), centred_to(N, k + 1))
                if k >= 2:
                    act.wait_ge(S("norm_square_used"), tiles_to(N, k - 1))
                act.activation(T[k % 2], src(k), ACT.Square).then_inc(S("norm_square"), 1)
            act.wait_ge(S("norm_square_used"), tiles_to(N, kts))
            act.activation(T[2], two(2), ACT.Sqrt, bias=eps[:, epscol:epscol + 1]).then_inc(S("norm_std"), 1)
            for k in range(kts):
                act.wait_ge(S("norm_scaled"), tiles_to(N, k + 1))
                if bias is None:
                    act.activation(dst(k), dst(k), ACT.Copy, scale=gain(k)).then_inc(S("norm_ready"), 1)
                else:
                    act.activation(dst(k), dst(k), ACT.Identity, scale=gain(k), bias=bias(k))\
                        .then_inc(S("norm_ready"), 1)

        def norm_dve(dve, N, kts, src, dst, centered, T):
            if centered:
                dve.wait_ge(S("norm_mean"), centred_to(N, FT) // FT)
                for k in range(kts):
                    dve.tensor_tensor(src(k), src(k), two(0), ALU.subtract).then_inc(S("norm_centred"), 1)
            dve.wait_ge(S("norm_std"), norms_to(N))
            dve.reciprocal(T[2], T[2]).then_inc(S("norm_rstd"), 1)
            dve.wait_ge(S("norm_rstd"), norms_to(N))
            for k in range(kts):
                dve.tensor_tensor(dst(k), src(k), T[2], ALU.mult).then_inc(S("norm_scaled"), 1)


        TEMPS_1 = (page(24), page(25), page(26))
        TEMPS_2 = (page(44), page(45), page(46))
        TEMPS_3 = (page(12), page(13), page(14))

        BLOCKS_WIN = 32
        B_UKV, B_UQ, B_GLU, B_PP = 32, 33, 35, 37
        B_WOUT = 39
        B_WPG = B_WOUT + 16
        B_QK1 = B_WPG + 16
        B_V1 = B_QK1 + 16
        B_QK2 = B_V1 + 4
        B_V2 = B_QK2 + 16
        B_MERGE = B_V2 + 4
        B_WOUT2 = B_MERGE + 24
        B_UP = B_WOUT2 + 8
        B_DOWN = B_UP + 44

        @block.sync
        def _(sp):
            def load(b, q, src, cols=PAGE):
                sp.dma_start(ring[:, b % RING, 0:cols], src).then_inc(S(f"w_landed{b % RING}"), 16)

            def loads(base, first, srcs):
                for j, (src, cols) in enumerate(srcs):
                    if not (isinstance(first, int) and first + j < RING):
                        sp.wait_ge(S("w_used"), first + (j - RING + 1))
                    load(base + j, None, src, cols)

            def tile_of(w, m):
                return (w[bass.ds(m, 1)].rearrange("a p n -> (a p) n"), w.shape[2])

            def w_in_blocks(i):
                out_ = []
                for j in range(4):
                    out_ += [tile_of(t["w_in"], i * 4 + j), tile_of(t["w_ada"], i * 4 + j)]
                return out_

            loads(0, 0, w_in_blocks(0))
            with sp.Fori(1, 4) as i:
                loads(0, i * 8, w_in_blocks(i))
            loads(B_UKV, B_UKV, [tile_of(t["w_ukv"], 0)])
            loads(B_UQ, B_UQ, [tile_of(t["w_uq"], m) for m in range(2)])
            loads(B_GLU, B_GLU, [tile_of(t["w_glu"], m) for m in range(2)])
            loads(B_PP, B_PP, [tile_of(t["w_pp"], m) for m in range(2)])

            def with_ada(base, w, m0, ada0, its):
                with sp.Fori(0, its) as i:
                    blocks_ = []
                    for j in range(4):
                        blocks_ += [tile_of(w, i * 4 + (m0 + j)), tile_of(t["w_ada"], i * 4 + (ada0 + j))]
                    loads(base, i * 8 + base, blocks_)

            with_ada(B_WOUT, t["w_out"], 0, 16, 2)
            with_ada(B_WPG, t["w_pg"], 0, 24, 2)
            if debug != 1:
                def half_tile(w, m, c0, c1):
                    return (w[bass.ds(m, 1), :, c0:c1].rearrange("a p n -> (a p) n"), c1 - c0)

                with_ada(B_QK1, t["w_qk_dil"], 0, 32, 2)
                loads(B_V1, B_V1, [tile_of(t["w_v_dil"], b) for b in range(4)])
                with_ada(B_QK2, t["w_qk_na"], 0, 40, 2)
                loads(B_V2, B_V2, [tile_of(t["w_v_na"], b) for b in range(4)])
                with sp.Fori(0, 2) as i:
                    loads(B_MERGE, i * 12 + B_MERGE,
                          [w for j in range(4) for w in (tile_of(t["w_gates"], i * 8 + 2 * j),
                                                         tile_of(t["w_gates"], i * 8 + (2 * j + 1)),
                                                         tile_of(t["w_branch"], i * 4 + j))])
                with sp.Fori(0, 2) as i:
                    loads(B_WOUT2, i * 4 + B_WOUT2, [tile_of(t["w_out_2"], i * 4 + j) for j in range(4)])
                with sp.Fori(0, N_UP // 2) as i:
                    loads(B_UP, i * 4 + B_UP, [tile_of(t["w_up"], i * 4 + j) for j in range(4)])
                with sp.Fori(0, 2) as i:
                    loads(B_DOWN, i * 12 + B_DOWN,
                          [half_tile(t["w_down"], i * 4 + j, 1024 * part, min(1024 * (part + 1), 22 * P))
                           for j in range(4) for part in range(3)])
            for k in range(FT):
                sp.wait_ge(S("norm_ready"), tiles_to("ln_1" if debug == 1 else "final", k + 1))
                sp.dma_start(out[k * P:(k + 1) * P, :], X2[:, k, :]).then_inc(S("out_written"), 16)
            sp.wait_ge(S("out_written"), 16 * FT)

        @block.gpsimd
        def _(pool):
            pool.memset(TM, 0.0).then_inc(S("tm_zero"), 1)
            pool.wait_ge(S("tm_zero"), 1)
            pool.wait_ge(S("g_skip"), 1)
            for s in range(STEP):
                pool.dma_start(TM[s * GC:(s + 1) * GC, :, s * GC:P], GSB[0:GC, :, 0:P - s * GC])\
                    .then_inc(S("tm_landed"), 16)
            pool.wait_ge(S("tables_built"), 1)
            pool.wait_ge(S("x_in_dram"), 16)
            for s in range(STEP):
                pool.dma_start(UU[s * GC:(s + 1) * GC, :, :],
                               x_dram.rearrange("(g c) t -> c g t", c=GC)[:, :, s * CHUNKS:(s + 1) * CHUNKS])\
                    .then_inc(S("u_landed"), 16)
            pool.wait_ge(S("states_ready"), 1)
            pool.dma_start(page(47).bitcast(I32), t["pos"].partition_broadcast(P)).then_inc(S("pos_landed"), 16)
            pool.wait_ge(S("ssm_ps_read"), 32)
            for s in range(STEP):
                pool.dma_start(y_dram.rearrange("(g c) t -> c g t", c=GC)[:, :, s * CHUNKS:(s + 1) * CHUNKS],
                               UU[s * GC:(s + 1) * GC, :, :]).then_inc(S("y_in_dram"), 16)
            pool.wait_ge(S("y_in_dram"), 16 * STEP)
            pool.dma_start(YF, y_dram.rearrange("(k p) t -> p k t", p=P)).then_inc(S("yf_landed"), 16)
            pool.wait_ge(S("cm_zero"), 1)
            pool.dma_start(CM[:, SEQ - P:SEQ], t["causal"]).then_inc(S("cm_landed"), 16)
            pool.wait_ge(S("norm_ready"), tiles_to("q_norm", 2))
            for half in range(2):
                pool.dma_start(page(46)[64 * half:64 * half + 64, :], KR[0:64, :]).then_inc(S("kr_landed"), 16)
                pool.dma_start(page(47)[64 * half:64 * half + 64, :], KR[64:128, :]).then_inc(S("kr_landed"), 16)
            pool.wait_ge(S("mla_out"), 32)
            pool.dma_start(PT_IN, t["pT"].rearrange("(k p) t -> p k t", p=P)).then_inc(S("p_landed"), 16)
            if debug == 1:
                return
            pool.memset(relb[0:33, :], 1.0).then_inc(S("relb_ones"), 1)
            pool.wait_ge(S("relb_ones"), 1)
            pool.dma_start(relb[0:32, :], t["rel_bias"]).then_inc(S("relb_landed"), 16)
            pool.wait_ge(S("kr_landed"), 64)
            pool.wait_ge(S("mla_out_read"), 32)
            pool.dma_start(page(20, 2)[0:33, :], t["onehot"]).then_inc(S("onehot_landed"), 16)
            pool.wait_ge(S("norm_scaled"), tiles_to("rms_mix", FT))
            pool.memset(page(12, 8), 0.0).then_inc(S("dil_q_zero"), 1)
            pool.wait_ge(S("dist_in_dram"), 16)
            for h in range(HEADS2):
                if h >= 2:
                    pool.wait_ge(S("dil_scores_read"), scores_used(*dil_items(), 8 * (h - 2) + 7))
                pool.dma_start(TB[h % 2], bass.AP(dist_dram.tensor, h * 2048, [[1, P], [1, 1920]]))\
                    .then_inc(S(f"dist_table{h % 2}"), 16)
            pool.wait_ge(S("dil_scores_read"), 64 + 4)
            pool.memset(page(12)[64:P, :], 0.0).then_inc(S("na_q_zero"), 1)
            pool.dma_start(COLM, t["na_masks"][:, 0:64]).then_inc(S("na_masks_landed"), 16)
            pool.dma_start(ROWM, t["na_masks"][:, 64:704]).then_inc(S("na_masks_landed"), 16)
            pool.wait_ge(S("na_masks_landed"), 32)
            pool.wait_ge(S("na_q_zero"), 1)
            for h in range(HEADS2):
                if h >= 2:
                    pool.wait_ge(S("na_scores_read"), scores_used(*na_items(), 8 * (h - 2) + 7))
                for rr in range(2):
                    src = bass.AP(t["rpb"].tensor, (15 * h + rr) * P, [[1, 64], [P, 14], [1, 64]])
                    pool.dma_start(NB[h % 2][64 * rr:64 * rr + 64, 0:896].rearrange("p (e c) -> p e c", c=64),
                                   src).then_inc(S(f"na_bias{h % 2}"), 16)
                pool.wait_ge(S(f"na_bias{h % 2}"), 32 * (h // 2 + 1))
                if h:
                    pool.wait_ge(S("na_table"), 2 * h)
                u = NB[h % 2][:, 0:896].rearrange("p (e c) -> p e c", c=64)
                pool.tensor_tensor(u, u, COLM.unsqueeze(1).to_broadcast((P, 14, 64)), ALU.add)\
                    .then_inc(S("na_table"), 1)
                pool.wait_ge(S("na_table"), 2 * h + 1)
                pool.tensor_tensor(NB[h % 2][:, 896:1536], NB[h % 2][:, 128:768], ROWM, ALU.add)\
                    .then_inc(S("na_table"), 1)

        @block.scalar
        def _(act):
            for h in range(4):
                act.dma_start(XN[:, 2 * h:2 * h + 2, :], t["xT"].rearrange("(k p) t -> p k t", p=P)
                              [:, 2 * h:2 * h + 2, :]).then_inc(S(f"x_landed{h}"), 16)
            act.dma_start(vec[:], t["vec"]).then_inc(S("vec_landed"), 16)
            act.dma_start(ident[:], t["ident"]).then_inc(S("ident_landed"), 16)
            act.dma_start(small[:, 0:3 * PAIRS], t["ssm"][:, 0:3 * PAIRS]).then_inc(S("ssm_landed"), 16)
            act.dma_start(BC, t["ssm"][:, 3 * PAIRS:].rearrange("p (i q c) -> p i q c", i=4, q=PAIRS))\
                .then_inc(S("bc_landed"), 16)
            act.dma_start(dsk[0:GC, :], t["dsk"]).then_inc(S("dsk_landed"), 16)
            act.dma_start(rope_c[:], t["rope_c"]).then_inc(S("rope_c_landed"), 16)
            act.wait_ge(S("vec_landed"), 16)
            act.activation(csilu[:], VV("c"), ACT.Silu).then_inc(S("c_ready"), 1)
            act.wait_ge(S("ssm_landed"), 16)
            act.activation(sm(3), sm(2), ACT.Exp).then_inc(S("dt_ready"), 1)
            act.wait_ge(S("dt_are"), 1)
            act.activation(sm(6), sm(4), ACT.Exp).then_inc(S("mag_ready"), 1)
            act.wait_ge(S("theta_reduced"), 1)
            act.activation(sm(7), sm(5), ACT.Sin).then_inc(S("sin_ready"), 1)
            act.activation(sm(8), sm(5), ACT.Sin, scale=0.5).then_inc(S("sin_ready"), 1)
            act.wait_ge(S("eps_set"), 2)
            norm_act(act, "ln_emb", FT, lambda k: XN[:, k, :], lambda k: XN[:, k, :],
                     lambda k: V("ln_emb_g", k), lambda k: V("ln_emb_b", k), 0, True, TEMPS_1)

            def z(tile, dst, func):
                act.wait_ge(S("z_tile"), tile + 1)
                src = two(2 * (tile % 2))
                if tile < 4:
                    dst = dst.rearrange("p (s n) -> p n s", s=STEP)
                    src = src.rearrange("p (n s) -> p n s", s=STEP)
                act.activation(dst, src, func).then_inc(S("z_free"), 1)

            def ada_read(group, last_block):
                act.wait_ge(S("w_used"), last_block + 1)
                act.activation(ada_raw[:, 4 * group:4 * group + 4], ps[:, 4, 0:4], ACT.Copy)\
                    .then_inc(S("ada_read"), 1)

            for tile in range(4):
                z(tile, XS[:, tile, :], ACT.Copy)
            ada_read(0, 7)
            act.wait_ge(S("z_free"), 4)
            act.dma_start(x_dram.rearrange("(k p) t -> p k t", p=P), XS).then_inc(S("x_in_dram"), 16)
            for tile in range(4, 8):
                z(tile, GS[:, tile - 4, :], ACT.Silu)
            ada_read(1, 15)
            for x in range(8):
                act.wait_ge(S("ssm_ps"), x + 1)
                act.activation(PW[:, 2 * x:2 * x + 2, :, :].rearrange("p q i n -> p (q i n)"),
                               ps[:, 5 + x % 2, :], ACT.Copy).then_inc(S("ssm_ps_read"), 1)
            for x in range(8, 16):
                r, odd = (x - 8) // 2, x % 2
                act.wait_ge(S("ssm_ps"), x + 1)
                act.activation(GSB[0:GC, 8 * r + odd:8 * r + 8:2, :],
                               ps[0:GC, 5 + x % 2, :].rearrange("p (g n) -> p g n", g=4), ACT.Copy)\
                    .then_inc(S("ssm_ps_read"), 1)
            for tile in range(8, 12):
                z(tile, CQ[:, tile - 8, :] if tile < 10 else (CKV if tile == 10 else KR), ACT.Copy)
            ada_read(2, 23)
            act.wait_ge(S("u_landed"), 16 * STEP)
            for x in range(16, 24):
                q4, i = (x - 16) // 2, x % 2
                act.wait_ge(S("ssm_ps"), x + 1)
                act.activation(SS[:, i, 4 * q4:4 * q4 + 4, :].rearrange("p q n -> p (q n)"),
                               ps[:, 5 + x % 2, :], ACT.Copy).then_inc(S("ssm_ps_read"), 1)
            act.wait_ge(S("tm_landed"), 16 * STEP)
            for tile in range(12, 16):
                z(tile, GM[:, tile - 12, :], ACT.Silu)
            ada_read(3, 31)
            act.wait_ge(S("angle_reduced"), 1)
            act.activation(SIN, COS, ACT.Sin).then_inc(S("rope_sin"), 1)
            act.activation(page(47), COS, ACT.Sin, scale=0.5).then_inc(S("rope_sin"), 1)
            for x in range(24, 32):
                r, odd = (x - 24) // 2, x % 2
                act.wait_ge(S("ssm_ps"), x + 1)
                act.activation(UU[:, 8 * r + odd:8 * r + 8:2, :],
                               ps[:, 5 + x % 2, :].rearrange("p (g n) -> p g n", g=4), ACT.Copy)\
                    .then_inc(S("ssm_ps_read"), 1)
            norm_act(act, "kv_norm", 1, lambda k: CKV, lambda k: CKV, lambda k: V("kv_norm_g", 0), None,
                     1, False, TEMPS_2)
            norm_act(act, "q_norm", 2, lambda k: CQ[:, k, :], lambda k: CQ[:, k, :],
                     lambda k: V("q_norm_g", k), None, 1, False, TEMPS_2)
            act.wait_ge(S("yf_landed"), 16)
            for m in range(4):
                act.wait_ge(S("kv_tile"), m + 1)
                act.activation(KN[:, m, :], two(2 * (m % 2)), ACT.Copy).then_inc(S("kv_free"), 1)
            for kt in range(8):
                act.wait_ge(S("kv_tile"), 4 + kt + 1)
                act.activation(VT[:, kt, :], ps[:, kt % 4, :], ACT.Copy).then_inc(S("kv_free"), 1)
            for m in range(4):
                act.wait_ge(S("q_tile"), m + 1)
                act.activation(QN[:, m, :], two(2 * (m % 2)), ACT.Copy).then_inc(S("q_free"), 1)
            for k in range(4):
                act.activation(YF[:, k, :], YF[:, k, :], ACT.Gelu_apprx_tanh).then_inc(S("yg_ready"), 1)
            for m in range(4):
                act.wait_ge(S("glu_tile"), m + 1)
                if m >= 2:
                    act.wait_ge(S("glu_used"), m - 1)
                act.activation(page(20 + m % 2), two(2 * (m % 2)), ACT.Sigmoid, bias=V("b_glu", m))\
                    .then_inc(S("glu_sig"), 1)
            act.wait_ge(S("glu_used"), 4)
            attention_act(act, "mla", BUFS_1, mla_items()[0], MLA_SCALE)
            for m in range(8):
                act.wait_ge(S("pp_tile"), m + 1)
                act.activation(PP[:, m, :], two(2 * (m % 2)), ACT.Copy).then_inc(S("pp_free"), 1)
            ada_read(4, B_WOUT + 7)
            ada_read(5, B_WOUT + 15)
            for m in range(8):
                if m == 4:
                    ada_read(6, B_WPG + 7)
                act.wait_ge(S("pg_tile"), m + 1)
                if m >= 2:
                    act.wait_ge(S("ple_ready"), m - 1)
                act.activation(page(24 + m % 2), two(2 * (m % 2)), ACT.Sigmoid).then_inc(S("pg_free"), 1)
            ada_read(7, B_WPG + 15)
            norm_act(act, "ln_1", FT, lambda k: X2[:, k, :], lambda k: X2[:, k, :],
                     lambda k: V("ln_g", k), lambda k: V("ln_b", k), 0, True, TEMPS_3)
            if debug == 1:
                return
            act.wait_ge(S("gains_1"), 1)
            act.wait_ge(S("norm_ready"), tiles_to("ln_1", FT))
            norm_act(act, "rms_mix", FT, lambda k: X2[:, k, :], lambda k: XN[:, k, :],
                     lambda k: gains[:, k:k + 1], lambda k: ada[:, k:k + 1], 1, False, TEMPS_3)
            for x in range(4):
                act.wait_ge(S("dist_tile"), x + 1)
                act.activation(page(22, 2)[0:HEADS2, x * BANK:(x + 1) * BANK], ps[0:HEADS2, 4 + x, :],
                               ACT.Copy).then_inc(S("dist_free"), 1)
            act.wait_ge(S("dist_free"), 4)
            act.dma_start(dist_dram, page(22, 2)[0:HEADS2, :]).then_inc(S("dist_in_dram"), 16)

            def qk_tiles(A, group, base):
                act.wait_ge(S(f"{A}_q_zero"), 1)
                for m in range(8):
                    act.wait_ge(S(f"{A}_qk_tile"), m + 1)
                    src = two(2 * (m % 2))
                    if m < 4:
                        for i in range(2):
                            h = slice(64 * i, 64 * i + 64)
                            ins = act.activation(Q2[h, 2 * m + i, :], src[h, :], ACT.Copy, scale=HD ** -0.5)
                        ins.then_inc(S(f"{A}_qk_free"), 1)
                    else:
                        if A == "dil" and m == 6:
                            act.wait_ge(S("dist_in_dram"), 16)
                        act.activation(K2[:, m - 4, :], src, ACT.Copy).then_inc(S(f"{A}_qk_free"), 1)
                    if m % 4 == 3:
                        ada_read(group + m // 4, base + 8 * (m // 4) + 7)

            def v_tiles(A):
                act.wait_ge(S(f"{A}_v_tiles"), 8)
                for k in range(4):
                    act.activation(V2[:, k, :], ps[:, k, :], ACT.Copy).then_inc(S(f"{A}_v_act"), 1)

            qk_tiles("dil", 8, B_QK1)
            v_tiles("dil")
            attention_act(act, "dil", BUFS_2, dil_items()[0], 1.0)
            qk_tiles("na", 10, B_QK2)
            v_tiles("na")
            attention_act(act, "na", BUFS_2, na_items()[0], 1.0)

            def merge_body(i):
                for j in range(4):
                    for half in range(2):
                        act.wait_ge(S("gate_tile"), i * 8 + (2 * j + half + 1))
                        if not (isinstance(i, int) and i == 0 and j < 2):
                            act.wait_ge(S("gate_used"), i * 4 + (j - 1))
                        act.activation(GT[:, 2 * (j % 2) + half, :], two(2 * half), ACT.Sigmoid)\
                            .then_inc(S("gate_free"), 1)
            merge_body(0)
            with act.Fori(1, 2) as i:
                merge_body(i)
            act.wait_ge(S("gains_2"), 1)
            act.wait_ge(S("x3_ready"), 8)
            norm_act(act, "rms_ffn", FT, lambda k: X2[:, k, :], lambda k: XN[:, k, :],
                     lambda k: gains[:, 8 + k:9 + k], lambda k: ada[:, 24 + k:25 + k], 1, False, TEMPS_3)

            def up_body(i):
                for j in range(2):
                    for half in range(2):
                        act.wait_ge(S("up_tile"), i * 4 + (2 * j + half + 1))
                        if not (isinstance(i, int) and i == 0):
                            act.wait_ge(S("ffn_ready"), i * 2 + (j - 1))
                        n = i * 2 + j
                        act.activation(UPB[:, 2 * j + half, :], two(4 * j + 2 * half), ACT.Identity,
                                       scale=one(conv, n + (2 + half) * N_UP),
                                       bias=one(conv, n + (6 + half) * N_UP)).then_inc(S("up_centre"), 1)
                    act.wait_ge(S("up_taps"), i * 4 + (2 * j + 2))
                    act.activation(UPB[:, 2 * j + 1, :], UPB[:, 2 * j + 1, :], ACT.Gelu_apprx_tanh)\
                        .then_inc(S("up_gelu"), 1)
            up_body(0)
            with act.Fori(1, N_UP // 2) as i:
                up_body(i)
            act.wait_ge(S("x4_ready"), 8)
            norm_act(act, "final", FT, lambda k: X2[:, k, :], lambda k: X2[:, k, :],
                     lambda k: V("g_final", k), None, 1, False, TEMPS_4)

        @block.vector
        def _(dve):
            chain = [0]

            def link(ins):
                chain[0] += 1
                ins.then_inc(S("dve_chain"), 1)
                dve.wait_ge(S("dve_chain"), chain[0])

            def tt(o, a, b, op):
                link(dve.tensor_tensor(o, a, b, op))

            def reduce_angle(a, n):
                link(dve.tensor_scalar(n, a, 1.0 / _TWO_PI, ROUND, ALU.mult, ALU.add))
                link(dve.tensor_scalar(n, n, ROUND, None, ALU.subtract))
                for part in (TP1, TP2, TP3):
                    link(dve.scalar_tensor_tensor(a, n, -part, a, ALU.mult, ALU.add))
                link(dve.tensor_scalar(a, a, PI_IN, -PI_IN, ALU.min, ALU.max))

            def cmul(ore, oim, are, aim, bre, bim, t1, t2):
                tt(t1, are, bre, ALU.mult)
                tt(t2, aim, bim, ALU.mult)
                tt(t1, t1, t2, ALU.subtract)
                tt(t2, are, bim, ALU.mult)
                tt(oim, aim, bre, ALU.mult)
                tt(oim, oim, t2, ALU.add)
                link(dve.tensor_copy(ore, t1))

            link(dve.memset(ones[:], 1.0 / D))
            link(dve.memset(ones_q[:], 1.0 / 256))
            link(dve.memset(ones_kv[:], 1.0 / 128))
            dve.memset(eps[:, 0:1], LN_EPS).then_inc(S("eps_set"), 1)
            dve.memset(eps[:, 1:2], RMS_EPS).then_inc(S("eps_set"), 1)
            dve.sem_inc(S("ones_set"), 1)
            dve.wait_ge(S("ssm_landed"), 16)
            dve.wait_ge(S("dt_ready"), 1)
            dve.tensor_tensor(sm(4), sm(3), sm(0), ALU.mult).then_inc(S("dt_are"), 1)
            tt(sm(5), sm(3), sm(1), ALU.mult)
            reduce_angle(sm(5), sm(9))
            dve.sem_inc(S("theta_reduced"), 1)
            norm_dve(dve, "ln_emb", FT, lambda k: XN[:, k, :], lambda k: XN[:, k, :], True, TEMPS_1)
            dve.wait_ge(S("sin_ready"), 2)
            dve.wait_ge(S("mag_ready"), 1)
            tt(sm(9), sm(8), sm(8), ALU.mult)
            link(dve.tensor_scalar(sm(8), sm(9), -2.0, 1.0, ALU.mult, ALU.add))
            PT = ptab[:].rearrange("p (i q j) -> p i q j", i=2, q=PAIRS)
            pre, pim = PT[:, 0], PT[:, 1]
            link(dve.memset(pre[:, :, 0], 1.0))
            link(dve.memset(pim[:, :, 0], 0.0))
            tt(pre[:, :, 1], sm(6), sm(8), ALU.mult)
            tt(pim[:, :, 1], sm(6), sm(7), ALU.mult)
            tt(sm(9), sm(0), sm(0), ALU.mult)
            tt(sm(10), sm(1), sm(1), ALU.mult)
            tt(sm(9), sm(9), sm(10), ALU.add)
            link(dve.reciprocal(sm(9), sm(9)))
            link(dve.tensor_scalar(sm(10), pre[:, :, 1], 1.0, None, ALU.subtract))
            tt(sm(11), sm(10), sm(0), ALU.mult)
            tt(sm(12), pim[:, :, 1], sm(1), ALU.mult)
            tt(sm(11), sm(11), sm(12), ALU.add)
            tt(sm(11), sm(11), sm(9), ALU.mult)
            tt(sm(12), pim[:, :, 1], sm(0), ALU.mult)
            tt(sm(13), sm(10), sm(1), ALU.mult)
            tt(sm(12), sm(12), sm(13), ALU.subtract)
            tt(sm(12), sm(12), sm(9), ALU.mult)
            def smalls(a, n):
                return arena[:, 28 * PAGE + a * 512:28 * PAGE + a * 512 + PAIRS * n]\
                    .rearrange("p (q n) -> p q n", q=PAIRS)
            for m in (1, 2, 4):
                last = slice(m, m + 1)
                cmul(pre[:, :, m + 1:2 * m + 1], pim[:, :, m + 1:2 * m + 1],
                     pre[:, :, 1:m + 1], pim[:, :, 1:m + 1],
                     pre[:, :, last].to_broadcast((P, PAIRS, m)), pim[:, :, last].to_broadcast((P, PAIRS, m)),
                     smalls(0, m), smalls(1, m))
            kre, kim = (sm(x).unsqueeze(2).to_broadcast((P, PAIRS, 8)) for x in (11, 12))
            ckre, ckim = smalls(4, 8), smalls(5, 8)
            cmul(ckre, ckim, pre[:, :, 0:8][:, :, ::-1], pim[:, :, 0:8][:, :, ::-1], kre, kim,
                 smalls(6, 8), smalls(7, 8))
            dve.wait_ge(S("bc_landed"), 16)

            def steps_by_channels(x, n):
                return x.unsqueeze(3).to_broadcast((P, PAIRS, n, GC))

            def channels_by_steps(x, n):
                return x.unsqueeze(2).to_broadcast((P, PAIRS, n, GC))

            def by_step(x, n):
                return x.rearrange("p q (s c) -> p q s c", c=GC)

            W0, W1 = by_step(WB[:, 0], 8), by_step(WB[:, 1], 8)
            ta = page(32, 2).rearrange("p (q s c) -> p q s c", q=PAIRS, c=GC)
            tb = page(34, 2).rearrange("p (q s c) -> p q s c", q=PAIRS, c=GC)
            B0, B1 = channels_by_steps(BC[:, 0], 8), channels_by_steps(BC[:, 1], 8)
            K0, K1 = steps_by_channels(ckre, 8), steps_by_channels(ckim, 8)
            tt(W0, K0, B0, ALU.mult)
            tt(ta, K1, B1, ALU.mult)
            tt(W0, W0, ta, ALU.subtract)
            tt(W1, K0, B1, ALU.mult)
            tt(tb, K1, B0, ALU.mult)
            tt(W1, W1, tb, ALU.add)
            dve.sem_inc(S("w_table"), 1)
            kre, kim = (sm(x).unsqueeze(2).to_broadcast((P, PAIRS, GC)) for x in (11, 12))
            cmul(KB[:, 0], KB[:, 1], BC[:, 0], BC[:, 1], kre, kim, smalls(6, 16), smalls(7, 16))
            C0, C1 = channels_by_steps(BC[:, 2], 9), channels_by_steps(BC[:, 3], 9)
            A0, A1 = steps_by_channels(pre, 9), steps_by_channels(pim, 9)
            Q0, Q1 = by_step(CP[:, 0], 9), by_step(CP[:, 1], 9)
            tc = arena[:, 28 * PAGE:28 * PAGE + PAIRS * 144].rearrange("p (q s c) -> p q s c", q=PAIRS, c=GC)
            tt(Q0, A0, C0, ALU.mult)
            tt(tc, A1, C1, ALU.mult)
            tt(Q0, Q0, tc, ALU.subtract)
            tt(Q1, A0, C1, ALU.mult)
            tt(tc, A1, C0, ALU.mult)
            tt(Q1, Q1, tc, ALU.add)
            link(dve.tensor_scalar(Q1, Q1, -1.0, None, ALU.mult))
            dve.sem_inc(S("cp_table"), 1)
            for x in range(3):
                tt(sm(6), sm(6), sm(6), ALU.mult)
                cmul(sm(8), sm(7), sm(8), sm(7), sm(8), sm(7), sm(9), sm(10))
            link(dve.memset(EE[:, 0, :, 0], 1.0))
            link(dve.memset(EE[:, 1, :, 0], 0.0))
            m = 1
            while m < CHUNKS:
                t1 = page(28, 1).rearrange("p (q n) -> p q n", q=PAIRS)[:, :, 0:m]
                t2 = page(29, 1).rearrange("p (q n) -> p q n", q=PAIRS)[:, :, 0:m]
                cmul(EE[:, 0, :, m:2 * m], EE[:, 1, :, m:2 * m], EE[:, 0, :, 0:m], EE[:, 1, :, 0:m],
                     sm(8).unsqueeze(2).to_broadcast((P, PAIRS, m)),
                     sm(7).unsqueeze(2).to_broadcast((P, PAIRS, m)), t1, t2)
                cmul(sm(8), sm(7), sm(8), sm(7), sm(8), sm(7), sm(9), sm(10))
                m *= 2
            dve.sem_inc(S("tables_built"), 1)
            dve.wait_ge(S("ssm_ps_read"), 16)
            dve.wait_ge(S("dsk_landed"), 16)
            dve.wait_ge(S("ident_landed"), 16)
            dg = arena[0:GC, _bc:_bc + GROUPS * GC].rearrange("p (g c) -> p g c", g=GROUPS)
            tt(dg, ident[0:GC, 0:GC].unsqueeze(1).to_broadcast((GC, GROUPS, GC)),
               dsk[0:GC, :].unsqueeze(2).to_broadcast((GC, GROUPS, GC)), ALU.mult)
            tt(GSB[0:GC, :, 0:GC], GSB[0:GC, :, 0:GC], dg, ALU.add)
            dve.sem_inc(S("g_skip"), 1)
            T1 = page(32, 2).rearrange("p (q n) -> p q n", q=PAIRS)
            T2 = page(34, 2).rearrange("p (q n) -> p q n", q=PAIRS)
            dve.wait_ge(S("ssm_ps_read"), 24)
            E0, E1, S0, S1 = EE[:, 0], EE[:, 1], SS[:, 0], SS[:, 1]
            tt(T1, S0, E1, ALU.mult)
            tt(T2, S1, E1, ALU.mult)
            tt(S0, S0, E0, ALU.mult)
            tt(S0, S0, T2, ALU.add)
            tt(T2, S1, E0, ALU.mult)
            tt(T2, T2, T1, ALU.subtract)
            for q in range(PAIRS):
                decay = sm(6)[:, q:q + 1].to_broadcast((P, CHUNKS))
                dve.tensor_tensor_scan(T1[:, q, :], decay, S0[:, q, :], 0.0, ALU.mult, ALU.add)\
                    .then_inc(S("scanned"), 1)
                dve.tensor_tensor_scan(S1[:, q, :], decay, T2[:, q, :], 0.0, ALU.mult, ALU.add)\
                    .then_inc(S("scanned"), 1)
            dve.wait_ge(S("scanned"), 2 * PAIRS)
            n1 = slice(0, CHUNKS - 1)
            tt(T2[:, :, n1], T1[:, :, n1], E0[:, :, n1], ALU.mult)
            tt(T1[:, :, n1], T1[:, :, n1], E1[:, :, n1], ALU.mult)
            tt(S0[:, :, 1:], S1[:, :, n1], E1[:, :, n1], ALU.mult)
            tt(S0[:, :, 1:], T2[:, :, n1], S0[:, :, 1:], ALU.subtract)
            tt(T2[:, :, n1], S1[:, :, n1], E0[:, :, n1], ALU.mult)
            tt(S1[:, :, 1:], T2[:, :, n1], T1[:, :, n1], ALU.add)
            link(dve.memset(S0[:, :, 0:1], 0.0))
            link(dve.memset(S1[:, :, 0:1], 0.0))
            dve.sem_inc(S("states_ready"), 1)
            pos_i = page(47).bitcast(I32)
            dve.wait_ge(S("pos_landed"), 16)
            link(dve.tensor_copy(COS, pos_i))
            dve.wait_ge(S("rope_c_landed"), 16)
            link(dve.tensor_scalar(COS, COS, rope_c[:, 0:1], None, ALU.mult))
            reduce_angle(COS, SIN)
            dve.sem_inc(S("angle_reduced"), 1)
            dve.wait_ge(S("rope_sin"), 2)
            link(dve.tensor_scalar(SIN, SIN, rope_c[:, 1:2], None, ALU.mult))
            tt(COS, page(47), page(47), ALU.mult)
            link(dve.tensor_scalar(COS, COS, -2.0, 1.0, ALU.mult, ALU.add))
            norm_dve(dve, "kv_norm", 1, lambda k: CKV, lambda k: CKV, False, TEMPS_2)
            norm_dve(dve, "q_norm", 2, lambda k: CQ[:, k, :], lambda k: CQ[:, k, :], False, TEMPS_2)
            dve.wait_ge(S("norm_ready"), tiles_to("q_norm", 2))
            link(dve.memset(CM, 0.0))
            dve.sem_inc(S("cm_zero"), 1)
            link(dve.memset(QR, 0.0))
            dve.wait_ge(S("kr_landed"), 64)
            tt(KROT, page(46), COS, ALU.mult)
            tt(page(46), page(47), SIN, ALU.mult)
            tt(KROT, KROT, page(46), ALU.add)
            for m in range(2):
                dve.wait_ge(S("qr_tile"), m + 1)
                for i in range(2):
                    h = slice(64 * i, 64 * i + 64)
                    tt(QR[h, 2 * m + i, :], two(0)[h, :], COS[h, :], ALU.mult)
                tt(page(46), two(2), SIN, ALU.mult)
                dve.sem_inc(S("qr_free"), 1)
                for i in range(2):
                    h = slice(64 * i, 64 * i + 64)
                    tt(QR[h, 2 * m + i, :], QR[h, 2 * m + i, :], page(46)[h, :], ALU.add)
            dve.sem_inc(S("rotary_ready"), 1)
            for m in range(4):
                dve.wait_ge(S("glu_sig"), m + 1)
                tt(page(20 + m % 2), page(20 + m % 2), YF[:, m, :], ALU.mult)
                link(dve.tensor_tensor(GS[:, m, :].rearrange("p (n s) -> p s n", s=STEP),
                                       GS[:, m, :].rearrange("p (n s) -> p s n", s=STEP),
                                       page(20 + m % 2).rearrange("p (s n) -> p s n", s=STEP), ALU.mult))
                dve.sem_inc(S("glu_used"), 1)
            dve.wait_ge(S("cm_landed"), 16)
            attention_dve(dve, "mla", BUFS_1, *mla_items(), MLA_SCALE, lambda i: None)
            for i in range(2):
                for j in range(4):
                    m = 4 * i + j
                    dve.wait_ge(S("wo_tile"), m + 1)
                    dve.scalar_tensor_tensor(XN[:, m, :], XN[:, m, :], ALPHA, two(2 * (m % 2)),
                                             ALU.mult, ALU.add).then_inc(S("u_ready"), 1)
            for i in range(2):
                for j in range(4):
                    m = 4 * i + j
                    dve.wait_ge(S("pg_free"), m + 1)
                    tt(page(24 + m % 2), page(24 + m % 2), PP[:, m, :], ALU.mult)
                    dve.tensor_tensor(X2[:, m, :], XN[:, m, :], page(24 + m % 2), ALU.add)\
                        .then_inc(S("ple_ready"), 1)
            dve.wait_ge(S("ple_ready"), 8)
            norm_dve(dve, "ln_1", FT, lambda k: X2[:, k, :], lambda k: X2[:, k, :], True, TEMPS_3)
            if debug == 1:
                return
            dve.wait_ge(S("ada_read"), 8)
            tt(ada[:, 0:32], ada_raw[:, 0:32], VV("b_ada")[:, 0:32], ALU.add)
            link(dve.scalar_tensor_tensor(gains[:, 0:8], ada[:, 8:16], 1.0, VV("g_mix"), ALU.add, ALU.mult))
            dve.sem_inc(S("gains_1"), 1)
            norm_dve(dve, "rms_mix", FT, lambda k: X2[:, k, :], lambda k: XN[:, k, :], False, TEMPS_3)

            def v_tiles(A):
                dve.wait_ge(S(f"{A}_v_tiles"), 8)
                for k in range(4, 8):
                    dve.tensor_copy(V2[:, k, :], ps[:, k, :]).then_inc(S(f"{A}_v_dve"), 1)

            def dil_table(i):
                if i % 8 == 0:
                    dve.wait_ge(S(f"dist_table{i // 8 % 2}"), 16 * (i // 16 + 1))

            def na_table(i):
                if i % 8 == 0:
                    dve.wait_ge(S("na_table"), 2 * (i // 8) + 2)
            v_tiles("dil")
            attention_dve(dve, "dil", BUFS_2, *dil_items(), 1.0, dil_table)
            v_tiles("na")
            attention_dve(dve, "na", BUFS_2, *na_items(), 1.0, na_table)
            dve.wait_ge(S("ada_read"), 12)
            tt(ada[:, 32:48], ada_raw[:, 32:48], VV("b_ada")[:, 32:48], ALU.add)
            link(dve.scalar_tensor_tensor(gains[:, 8:16], ada[:, 32:40], 1.0, VV("g_ffn"), ALU.add, ALU.mult))
            dve.sem_inc(S("gains_2"), 1)

            def merge_body(i):
                for j in range(4):
                    a, b = GT[:, 2 * (j % 2), :], GT[:, 2 * (j % 2) + 1, :]
                    dve.wait_ge(S("gate_free"), i * 8 + (2 * j + 2))
                    dve.wait_ge(S("branch_tile"), i * 4 + (j + 1))
                    dve.tensor_tensor(a, a, two(4), ALU.mult).then_inc(S("branch_read"), 1)
                    dve.tensor_tensor(b, b, two(6), ALU.mult).then_inc(S("branch_read"), 1)
                    dve.wait_ge(S("branch_read"), i * 8 + (2 * j + 2))
                    dve.tensor_tensor(pg(MRG, i * 4 + j), a, b, ALU.add).then_inc(S("gate_used"), 1)
            with dve.Fori(0, 2) as i:
                merge_body(i)
            with dve.Fori(0, 2) as i:
                for j in range(4):
                    dve.wait_ge(S("wo2_tile"), i * 4 + (j + 1))
                    x = pg(X2, i * 4 + j)
                    dve.scalar_tensor_tensor(x, two(2 * (j % 2)), one(ada, i * 4 + (16 + j)), x,
                                             ALU.mult, ALU.add).then_inc(S("x3_ready"), 1)
            dve.wait_ge(S("x3_ready"), 8)
            norm_dve(dve, "rms_ffn", FT, lambda k: X2[:, k, :], lambda k: XN[:, k, :], False, TEMPS_3)
            with dve.Fori(0, N_UP // 2) as i:
                for j in range(2):
                    n = i * 2 + j
                    for half in range(2):
                        y, src = UPB[:, 2 * j + half, :], two(4 * j + 2 * half)
                        dve.wait_ge(S("up_centre"), i * 4 + (2 * j + half + 1))
                        dve.scalar_tensor_tensor(y[:, 1:], src[:, :SEQ - 1],
                                                 one(conv, n + (half * N_UP)), y[:, 1:],
                                                 ALU.mult, ALU.add).then_inc(S("up_left"), 1)
                        dve.wait_ge(S("up_left"), i * 4 + (2 * j + half + 1))
                        dve.scalar_tensor_tensor(y[:, :SEQ - 1], src[:, 1:],
                                                 one(conv, n + ((4 + half) * N_UP)), y[:, :SEQ - 1],
                                                 ALU.mult, ALU.add).then_inc(S("up_taps"), 1)
                    dve.wait_ge(S("up_gelu"), i * 2 + (j + 1))
                    dve.tensor_tensor(pg(ACTV, n), UPB[:, 2 * j, :], UPB[:, 2 * j + 1, :], ALU.mult)\
                        .then_inc(S("ffn_ready"), 1)
            with dve.Fori(0, 2) as i:
                for j in range(4):
                    dve.wait_ge(S("down_tile"), i * 4 + (j + 1))
                    x = pg(X2, i * 4 + j)
                    dve.scalar_tensor_tensor(x, two(2 * (j % 2)), one(ada, i * 4 + (40 + j)), x,
                                             ALU.mult, ALU.add).then_inc(S("x4_ready"), 1)
            norm_dve(dve, "final", FT, lambda k: X2[:, k, :], lambda k: X2[:, k, :], False, TEMPS_4)

        @block.tensor
        def _(pe):
            def block_landed(b, q=None):
                pe.wait_ge(S(f"w_landed{b % RING}"), 16 * (b // RING + 1) if q is None else q * 16 + 16)

            def tile(bank, slot, rhs, kts=FT, at=0, start=True, stop=True, k0=0, step=P, give_back=False):
                for k in range(kts):
                    for nt in range(2):
                        mm = pe.matmul(ps[:, bank + nt, :], ring[:, slot, at + k * step:at + k * step + P],
                                       rhs(k0 + k)[:, nt * BANK:(nt + 1) * BANK],
                                       start=start and k == 0, stop=stop and k == kts - 1)
                        if give_back and k == 0 and nt == 0:
                            mm.then_inc(S("w_used"), 1)
                return mm

            def four_with_ada(i, base, group, done, free, rhs):
                for j in range(4):
                    b = base + 2 * j
                    block_landed(b, 2 * i + b // RING)
                    if not (isinstance(i, int) and i == 0) or j >= 2:
                        pe.wait_ge(S(free), 4 * i + (j - 1))
                    tile(2 * (j % 2), b % RING, rhs).then_inc(S(done), 1)
                    b += 1
                    block_landed(b, 2 * i + b // RING)
                    if j == 0 and not (isinstance(group, int) and group == 0):
                        pe.wait_ge(S("ada_read"), group)
                    for k in range(FT):
                        mm = pe.matmul(ps[:, 4, j:j + 1], ring[:, b % RING, k * P:(k + 1) * P],
                                       csilu[:, k:k + 1], start=k == 0, stop=k == FT - 1)
                        if k in (0, FT - 1):
                            mm.then_inc(S("w_used"), 1)

            pe.wait_ge(S("ones_set"), 1)
            for h in range(4):
                pe.wait_ge(S(f"x_landed{h}"), 16)
            norm_pe(pe, "ln_emb", FT, lambda k: XN[:, k, :], ones[:], True, TEMPS_1)
            pe.wait_ge(S("norm_ready"), tiles_to("ln_emb", FT))
            pe.wait_ge(S("c_ready"), 1)
            xn = lambda k: XN[:, k, :]
            four_with_ada(0, 0, 0, "z_tile", "z_free", xn)
            four_with_ada(1, 0, 1, "z_tile", "z_free", xn)
            pe.wait_ge(S("w_table"), 1)
            pe.wait_ge(S("ident_landed"), 16)
            for x in range(8):
                if x >= 2:
                    pe.wait_ge(S("ssm_ps_read"), x - 1)
                for j in range(4):
                    mm = pe.transpose(ps[:, 5 + x % 2, j * P:(j + 1) * P], WB[:, j % 2, 2 * x + j // 2, :],
                                      ident[:])
                mm.then_inc(S("ssm_ps"), 1)
            pe.wait_ge(S("cp_table"), 1)
            for x in range(8, 16):
                pe.wait_ge(S("ssm_ps_read"), x - 1)
                r, odd = (x - 8) // 2, x % 2
                h = slice(64 * odd, 64 * odd + 64)
                for j in range(4):
                    q = 4 * r + j
                    for i in range(2):
                        mm = pe.matmul(ps[0:GC, 5 + x % 2, j * P:(j + 1) * P], KB[h, i, q, :],
                                       CP[h, i, q, 0:P], start=i == 0, stop=i == 1)
                mm.then_inc(S("ssm_ps"), 1)
            four_with_ada(2, 0, 2, "z_tile", "z_free", xn)
            pe.wait_ge(S("u_landed"), 16 * STEP)
            for x in range(16, 24):
                pe.wait_ge(S("ssm_ps_read"), x - 1)
                q4, i = (x - 16) // 2, x % 2
                for j in range(4):
                    q = 4 * q4 + j
                    for g2 in range(2):
                        mm = pe.matmul(ps[64 * g2:64 * g2 + 64, 5 + x % 2, j * P:(j + 1) * P],
                                       PW[:, q, i, 64 * g2:64 * g2 + 64], UU[:, 2 * q + g2, :],
                                       start=True, stop=True)
                mm.then_inc(S("ssm_ps"), 1)
            four_with_ada(3, 0, 3, "z_tile", "z_free", xn)
            pe.wait_ge(S("states_ready"), 1)
            pe.wait_ge(S("tm_landed"), 16 * STEP)
            for x in range(24, 32):
                pe.wait_ge(S("ssm_ps_read"), x - 1)
                r, odd = (x - 24) // 2, x % 2
                h = slice(64 * odd, 64 * odd + 64)
                for j in range(4):
                    q = 4 * r + j
                    o = ps[:, 5 + x % 2, j * P:(j + 1) * P]
                    pe.matmul(o, TM[:, 2 * q + odd, :], UU[:, 2 * q + odd, :], start=True, stop=False)
                    for i in range(2):
                        mm = pe.matmul(o, CP[h, i, q, GC:GC + P], SS[h, i, q, :], start=False, stop=i == 1)
                mm.then_inc(S("ssm_ps"), 1)
            pe.wait_ge(S("z_free"), 16)
            norm_pe(pe, "kv_norm", 1, None, ones_kv[:], False, TEMPS_2)
            pe.wait_ge(S("norm_std"), norms_to("kv_norm"))
            norm_pe(pe, "q_norm", 2, None, ones_q[:], False, TEMPS_2)
            pe.wait_ge(S("norm_std"), norms_to("q_norm"))
            pe.wait_ge(S("norm_ready"), tiles_to("kv_norm", 1))
            b = B_UKV
            block_landed(B_UKV)
            for m in range(4):
                if m >= 2:
                    pe.wait_ge(S("kv_free"), m - 1)
                tile(2 * (m % 2), b % RING, lambda k: CKV, kts=1, at=m * P).then_inc(S("kv_tile"), 1)
            for kt in range(8):
                if kt == 0:
                    pe.wait_ge(S("kv_free"), 4)
                if kt >= 4:
                    pe.wait_ge(S("kv_free"), kt + 1)
                mm = pe.matmul(ps[:, kt % 4, :], CKV[:, kt * P:(kt + 1) * P], ring[:, b % RING, BANK:2 * BANK],
                               start=True, stop=True).then_inc(S("kv_tile"), 1)
            pe.wait_ge(S("kv_tile"), 12)
            pe.sem_inc(S("w_used"), 1)
            pe.wait_ge(S("norm_ready"), tiles_to("q_norm", 2))
            pe.wait_ge(S("kv_free"), 12)
            block_landed(B_UQ)
            for m in range(4):
                if m >= 2:
                    pe.wait_ge(S("q_free"), m - 1)
                mm = tile(2 * (m % 2), B_UQ % RING, lambda k: CQ[:, k, :], kts=2, at=m * P, step=BANK)
                mm.then_inc(S("q_tile"), 1)
            pe.wait_ge(S("q_tile"), 4)
            pe.sem_inc(S("w_used"), 1)
            block_landed(B_UQ + 1)
            pe.wait_ge(S("q_free"), 4)
            for m in range(2):
                if m == 1:
                    pe.wait_ge(S("qr_free"), 1)
                tile(0, (B_UQ + 1) % RING, lambda k: CQ[:, k, :], kts=2, at=m * P, step=BANK)
                tile(2, (B_UQ + 1) % RING, lambda k: CQ[:, k, :], kts=2, at=(2 + m) * P, step=BANK)\
                    .then_inc(S("qr_tile"), 1)
            pe.wait_ge(S("qr_tile"), 2)
            pe.sem_inc(S("w_used"), 1)
            pe.wait_ge(S("yg_ready"), 4)
            pe.wait_ge(S("qr_free"), 2)
            for m in range(4):
                block_landed(B_GLU + m // 2)
                if m >= 2:
                    pe.wait_ge(S("glu_sig"), m - 1)
                mm = tile(2 * (m % 2), (B_GLU + m // 2) % RING, lambda k: YF[:, k, :], kts=4,
                          at=(m % 2) * P, step=2 * P)
                mm.then_inc(S("glu_tile"), 1)
                if m % 2:
                    pe.wait_ge(S("glu_tile"), m + 1)
                    pe.sem_inc(S("w_used"), 1)
            pe.wait_ge(S("rotary_ready"), 1)
            pe.wait_ge(S("glu_sig"), 4)
            attention_pe(pe, "mla", BUFS_1, *mla_items())
            pe.wait_ge(S("mla_scores_read"), 32 + MLA_HEADS)
            pe.wait_ge(S("p_landed"), 16)
            for m in range(8):
                block_landed(B_PP + m // 4)
                if m >= 2:
                    pe.wait_ge(S("pp_free"), m - 1)
                mm = tile(2 * (m % 2), (B_PP + m // 4) % RING, lambda k: PT_IN[:, k, :], kts=2,
                          at=(m % 4) * P, step=BANK)
                mm.then_inc(S("pp_tile"), 1)
                if m % 4 == 3:
                    pe.wait_ge(S("pp_tile"), m + 1)
                    pe.sem_inc(S("w_used"), 1)
            pe.wait_ge(S("pp_free"), 8)
            mixed = lambda k: GS[:, k, :] if k < 4 else GM[:, k - 4, :]
            four_with_ada(0, B_WOUT, 4, "wo_tile", "u_ready", mixed)
            four_with_ada(1, B_WOUT, 5, "wo_tile", "u_ready", mixed)
            pe.wait_ge(S("u_ready"), 8)
            four_with_ada(0, B_WPG, 6, "pg_tile", "pg_free", xn)
            four_with_ada(1, B_WPG, 7, "pg_tile", "pg_free", xn)
            pe.wait_ge(S("ple_ready"), 8)
            norm_pe(pe, "ln_1", FT, lambda k: X2[:, k, :], ones[:], True, TEMPS_3)
            if debug == 1:
                return
            pe.wait_ge(S("norm_ready"), tiles_to("ln_1", FT))
            norm_pe(pe, "rms_mix", FT, None, ones[:], False, TEMPS_3)
            pe.wait_ge(S("relb_landed"), 16)
            pe.wait_ge(S("onehot_landed"), 16)
            for x in range(4):
                pe.matmul(ps[0:HEADS2, 4 + x, :], relb[0:33, :], page(20, 2)[0:33, x * BANK:(x + 1) * BANK],
                          start=True, stop=True).then_inc(S("dist_tile"), 1)
            pe.wait_ge(S("dist_free"), 4)
            pe.wait_ge(S("norm_ready"), tiles_to("rms_mix", FT))

            def qkv(A, base_qk, base_v, group):
                four_with_ada(0, base_qk, group, f"{A}_qk_tile", f"{A}_qk_free", xn)
                four_with_ada(1, base_qk, group + 1, f"{A}_qk_tile", f"{A}_qk_free", xn)
                pe.wait_ge(S(f"{A}_qk_free"), 8)
                pe.wait_ge(S("ada_read"), group + 2)
                for b in range(4):
                    block_landed(base_v + b)
                    for kt in range(8):
                        for k in range(2):
                            mm = pe.matmul(ps[:, kt, :], XN[:, 2 * b + k, kt * P:(kt + 1) * P],
                                           ring[:, (base_v + b) % RING, k * BANK:(k + 1) * BANK],
                                           start=b == 0 and k == 0, stop=b == 3 and k == 1)
                            if b > 0 and kt == 0 and k == 0:
                                mm.then_inc(S("w_used"), 1)
                        if b == 3:
                            mm.then_inc(S(f"{A}_v_tiles"), 1)
                pe.wait_ge(S(f"{A}_v_act"), 4)
                pe.wait_ge(S(f"{A}_v_dve"), 4)
                pe.sem_inc(S("w_used"), 1)

            qkv("dil", B_QK1, B_V1, 8)
            attention_pe(pe, "dil", BUFS_2, *dil_items())
            pe.wait_ge(S("dil_scores_read"), 64 + 4)
            pe.wait_ge(S("dil_out_read"), 64)
            qkv("na", B_QK2, B_V2, 10)
            attention_pe(pe, "na", BUFS_2, *na_items())
            pe.wait_ge(S("na_scores_read"), 64 + 4)
            pe.wait_ge(S("na_out_read"), 64)

            def turns_of(b, i, per):
                return i * (per // RING) + b // RING

            def merge_body(i):
                first = isinstance(i, int) and i == 0
                for j in range(4):
                    for half in range(2):
                        b = B_MERGE + 3 * j + half
                        block_landed(b, turns_of(b, i, 12))
                        if not (first and j == 0):
                            pe.wait_ge(S("gate_free"), i * 8 + (2 * j + half - 1))
                        mm = tile(2 * half, b % RING, xn, give_back=half == 1 or not (first and j == 0))
                        mm.then_inc(S("gate_tile"), 1)
                    b = B_MERGE + 3 * j + 2
                    block_landed(b, turns_of(b, i, 12))
                    if not (first and j == 0):
                        pe.wait_ge(S("branch_read"), i * 8 + 2 * j)
                    tile(4, b % RING, lambda k: OAT[:, k, :], kts=4, give_back=True)
                    tile(6, b % RING, lambda k: ONT[k], kts=4, at=4 * P).then_inc(S("branch_tile"), 1)
            merge_body(0)
            with pe.Fori(1, 2) as i:
                merge_body(i)
            pe.wait_ge(S("branch_tile"), 8)
            pe.sem_inc(S("w_used"), 1)
            pe.wait_ge(S("gate_free"), 16)
            pe.wait_ge(S("gate_used"), 8)

            def wo2_body(i):
                first = isinstance(i, int) and i == 0
                for j in range(4):
                    b = B_WOUT2 + j
                    block_landed(b, turns_of(b, i, 4))
                    if not (first and j < 2):
                        pe.wait_ge(S("x3_ready"), i * 4 + (j - 1))
                    tile(2 * (j % 2), b % RING, lambda k: MRG[:, k, :], give_back=not (first and j == 0))\
                        .then_inc(S("wo2_tile"), 1)
            wo2_body(0)
            with pe.Fori(1, 2) as i:
                wo2_body(i)
            pe.wait_ge(S("wo2_tile"), 8)
            pe.sem_inc(S("w_used"), 1)
            pe.wait_ge(S("x3_ready"), 8)
            norm_pe(pe, "rms_ffn", FT, None, ones[:], False, TEMPS_3)
            pe.wait_ge(S("norm_ready"), tiles_to("rms_ffn", FT))

            def up_body(i):
                first = isinstance(i, int) and i == 0
                for j in range(2):
                    for half in range(2):
                        b = B_UP + 2 * j + half
                        block_landed(b, turns_of(b, i, 4))
                        if not first:
                            pe.wait_ge(S("up_taps"), i * 4 + (2 * j + half - 3))
                        tile(4 * j + 2 * half, b % RING, xn, give_back=not (first and j == 0 and half == 0))\
                            .then_inc(S("up_tile"), 1)
            up_body(0)
            with pe.Fori(1, N_UP // 2) as i:
                up_body(i)
            pe.wait_ge(S("up_tile"), 2 * N_UP)
            pe.sem_inc(S("w_used"), 1)
            pe.wait_ge(S("ffn_ready"), N_UP)

            def down_body(i):
                first = isinstance(i, int) and i == 0
                for j in range(4):
                    for part, kts in enumerate((8, 8, 6)):
                        b = B_DOWN + 3 * j + part
                        block_landed(b, turns_of(b, i, 12))
                        if part == 0 and not (first and j < 2):
                            pe.wait_ge(S("x4_ready"), i * 4 + (j - 1))
                        mm = tile(2 * (j % 2), b % RING, lambda k: ACTV[:, k, :], kts=kts, k0=8 * part,
                                  start=part == 0, stop=part == 2,
                                  give_back=not (first and j == 0 and part == 0))
                    mm.then_inc(S("down_tile"), 1)
            down_body(0)
            with pe.Fori(1, 2) as i:
                down_body(i)
            pe.wait_ge(S("x4_ready"), 8)
            norm_pe(pe, "final", FT, None, ones[:], False, TEMPS_4)

DEBUG = 0


def kernel(**inputs):
    import numpy as _np
    import concourse.bacc as _bacc
    from concourse import mybir as _mybir
    from concourse.bass_utils import run_bass_kernel_spmd as _run

    g = {k: _np.asarray(v) for k, v in inputs.items()}

    def tiled(w, m=P):
        K, M = w.shape
        return _np.ascontiguousarray(w.reshape(K // P, P, M // m, m).transpose(2, 1, 0, 3)
                                     .reshape(M // m, P, K // P * m))

    def cols(v):
        return v.reshape(-1, P).T

    def halves(w):
        K, M = w.shape
        return w.reshape(K, M // 64, 2, 32)[:, :, ::-1].reshape(K, M)

    w_in = g["w_in"][0]
    xs, gs, cq, ckv, kr, gm = _np.split(w_in, _np.cumsum([512, 512, 256, 128, 64]).tolist(), axis=1)
    uq = g["w_uq"][0].reshape(256, MLA_HEADS, 192)
    uq_plain, uq_rot = uq[:, :, :P].reshape(256, 512), uq[:, :, P:].reshape(256, 256)
    ukv = g["w_ukv"][0].reshape(P, MLA_HEADS, 256)
    ukv = _np.concatenate([ukv[:, :, :P].reshape(P, 512), ukv[:, :, P:].reshape(P, 512)], axis=1)

    def pairs(a):
        a = a.reshape((PAIRS, 2, STATE) + a.shape[2:])
        return _np.moveaxis(a, 0, 2).reshape(P, -1)

    vec = _np.concatenate([cols(g[n].reshape(-1)) for n in (
        "ln_emb_g", "ln_emb_b", "b_glu", "q_norm_g", "kv_norm_g", "ln_g", "ln_b", "c_2", "b_ada_2",
        "g_mix_2", "g_ffn_2", "conv_w_2", "conv_b_2", "g_final_2")], axis=1)
    p_ = _np.arange(P)
    inv_freq = (1.0 / 10000.0 ** (2 * (p_ % 32) / 64.0)).astype(_np.float32)
    sign = _np.where(p_ % 64 < 32, -1.0, 1.0).astype(_np.float32)
    arrays = {
        "xT": g["x"][0].T, "pT": g["p"][0, 0].T, "pos": g["positions"].reshape(SEQ), "vec": vec,
        "ident": _np.eye(P, dtype=_np.float32),
        "causal": _np.where(p_[None, :] > p_[:, None], MASKED, 0.0).astype(_np.float32),
        "rope_c": _np.stack([inv_freq, sign], axis=1),
        "ssm": _np.concatenate([pairs(g["a_re"][0]), pairs(g["a_im"][0]),
                                pairs(_np.repeat(g["log_dt"][0][:, None], STATE, 1)),
                                pairs(g["b_re"][0]), pairs(g["b_im"][0]),
                                pairs(g["c_re"][0].transpose(0, 2, 1)), pairs(g["c_im"][0].transpose(0, 2, 1))],
                               axis=1),
        "dsk": g["d_skip"][0].reshape(GROUPS, GC).T,
        "w_in": tiled(_np.concatenate([xs, gs, cq, ckv, kr, halves(kr), gm], axis=1)),
        "w_ada": tiled(g["w_ada_2"][0]), "w_glu": tiled(g["w_glu"][0], 2 * P),
        "w_uq": tiled(_np.concatenate([uq_plain, uq_rot, halves(uq_rot)], axis=1), 512),
        "w_ukv": tiled(ukv, 1024), "w_pp": tiled(g["w_pp"][0], 512),
        "w_out": tiled(g["w_out"][0]), "w_pg": tiled(g["w_pg"][0]),
    }
    w2 = g["w_in_2"][0]
    dq, dk, dv, nq, nk, nv, ga, gb = _np.split(w2, _np.cumsum([512] * 6 + [1024]).tolist(), axis=1)

    def by_two(w):
        return w.reshape(4, 2, P, 512).transpose(0, 2, 1, 3).reshape(4, P, 1024)

    def alternate(a, b):
        a, b = (w.reshape(w.shape[0], -1, 1, P) for w in (a, b))
        return _np.concatenate([a, b], axis=2).reshape(a.shape[0], -1)

    d = 1023 - _np.arange(2048)
    a = _np.abs(d)
    large = 8 + (_np.log(_np.maximum(a, 1).astype(_np.float32) / 8) / math.log(1024 / 8) * 8).astype(_np.int32)
    bucket = _np.where(d > 0, 16, 0) + _np.where(a < 8, a, _np.minimum(large, 15))
    times = sum(((a % dil == 0) & (a <= win // 2)).astype(int) for win, dil in ((128, 1), (512, 4), (2048, 16)))
    onehot = _np.zeros((33, 2048), _np.float32)
    onehot[bucket, _np.arange(2048)] = 1.0
    onehot[32] = _np.where(times > 0, _np.log(_np.maximum(times, 1)), MASKED)
    cq_, ck_ = p_ % 64, 63 - _np.arange(64)
    start = _np.clip(cq_ - 8, 0, 48)
    colm = _np.where((ck_[None] >= start[:, None]) & (ck_[None] < start[:, None] + 16), 0.0, MASKED)
    dr_ = 5 - _np.arange(10)
    off = dr_[None] - (p_ // 64)[:, None]
    rowm = _np.repeat(_np.where((off >= -4) & (off <= 3), 0.0, MASKED), 64, axis=1)
    rpb = _np.zeros((8, 15, P), _np.float32)
    rpb[:, :, 48:79] = g["na_rpb_2"][0][:, ::-1, ::-1]
    arrays.update({
        "w_qk_dil": tiled(_np.concatenate([dq, dk], axis=1)), "w_v_dil": by_two(dv),
        "w_qk_na": tiled(_np.concatenate([nq, nk], axis=1)), "w_v_na": by_two(nv),
        "w_gates": tiled(alternate(ga, gb)),
        "w_branch": tiled(_np.concatenate([g["w_branch_dil_2"][0], g["w_branch_na_2"][0]], axis=0)),
        "w_out_2": tiled(g["w_out_2"][0]),
        "w_up": tiled(alternate(g["w_up_2"][0][:, :N_UP * P], g["w_up_2"][0][:, N_UP * P:])),
        "w_down": tiled(g["w_down_2"][0]),
        "rel_bias": g["rel_bias_2"], "onehot": onehot, "rpb": rpb.reshape(120, P),
        "na_masks": _np.concatenate([colm, rowm], axis=1).astype(_np.float32),
    } if DEBUG != 1 else {})
    arrays = {k: _np.ascontiguousarray(v) for k, v in arrays.items()}
    nc = _bacc.Bacc("TRN2", target_bir_lowering=False, num_devices=1)
    t = {n: nc.dram_tensor(n, a.shape, _mybir.dt.from_np(a.dtype), kind="ExternalInput").ap()
         for n, a in arrays.items()}
    out = nc.dram_tensor("out", (D, SEQ), F32, kind="ExternalOutput").ap()
    program(nc, t, out, DEBUG)
    r = _run(nc, [arrays], core_ids=[0])
    return _np.ascontiguousarray(r.results[0]["out"].T)[None]
```

```python
import math
from contextlib import ExitStack

import numpy as np

import concourse.bass as bass
from concourse import mybir

F32 = mybir.dt.float32
I32 = mybir.dt.int32
F32R = mybir.dt.float32r
ALU = mybir.AluOpType
ACT = mybir.ActivationFunctionType

P = 128
SEQ = 1024
D = 1024
FT = D // P
BANK = 512
PAGE = 1024
RING = 4
PAGES, FRONT = 50, 12
LN_EPS, RMS_EPS = 1e-5, 1e-6
ALPHA = 2.0 ** 0.25
MASKED = -1e30

GROUPS, GC, STATE = 32, 16, 64
PAIRS = GROUPS // 2
STEP = P // GC
CHUNKS = SEQ // STEP
MLA_HEADS = 4
MLA_SCALE = (128 + 64) ** -0.5
HEADS2, HD = 8, 64
N_UP = 22

_TWO_PI = 2 * math.pi
TP1 = float(np.float32(round(_TWO_PI * 2 ** 9) / 2 ** 9))
TP2 = float(np.float32(round((_TWO_PI - TP1) * 2 ** 22) / 2 ** 22))
TP3 = float(np.float32(_TWO_PI - TP1 - TP2))
ROUND = float(1.5 * 2 ** 23)
PI_IN = 3.1415925

VEC = {}
_at = 0
for _name, _n in (("ln_emb_g", 8), ("ln_emb_b", 8), ("b_glu", 4), ("q_norm_g", 2), ("kv_norm_g", 1),
                  ("ln_g", 8), ("ln_b", 8), ("c", 8), ("b_ada", 48), ("g_mix", 8), ("g_ffn", 8),
                  ("conv_w", 3 * 2 * N_UP), ("conv_b", 2 * N_UP), ("g_final", 8)):
    VEC[_name] = (_at, _n)
    _at += _n
N_VEC = _at


def program(nc, t, out):
    with ExitStack() as ctx:
        sems = {}

        def S(name):
            if name not in sems:
                sems[name] = ctx.enter_context(nc.semaphore(name))
            return sems[name]

        front = ctx.enter_context(nc.sbuf_tensor("front", [P, FRONT * PAGE], F32))
        back = ctx.enter_context(nc.sbuf_tensor("back", [P, (PAGES - FRONT) * PAGE], F32))
        pages_at = nc.sbuf_base - PAGES * PAGE * 4

        def cols(a, b, parts=P):
            if b <= FRONT * PAGE:
                return front[0:parts, a:b]
            return back[0:parts, a - FRONT * PAGE:b - FRONT * PAGE]

        def rounded_pages(name, a, n):
            return [nc.alloc_sbuf_tensor_at(f"{name}_{k}", [P, PAGE], F32R,
                                            offset=pages_at + (a + k) * PAGE * 4)[:, :] for k in range(n)]

        ps = ctx.enter_context(nc.psum_tensor("ps", [P, 8, BANK], F32))

        def sb(name, cols, dt=F32):
            return ctx.enter_context(nc.sbuf_tensor(f"sb_{name}", [P, cols], dt))

        def page(a, n=1, off=0):
            return cols(a * PAGE + off, (a + n) * PAGE + off)

        def pages(a, n):
            return page(a, n).rearrange("p (k t) -> p k t", k=n)

        def two(b):
            return ps[:, b:b + 2, :].rearrange("p a b -> p (a b)")

        vec = sb("vec", N_VEC)
        ident = sb("ident", P)
        ones = sb("ones", P)
        rope_c = sb("rope_c", 2)
        eps = sb("eps", 2)
        csilu = sb("csilu", 8)
        ada = sb("ada", 48)
        stat = sb("stat", 16)
        small = sb("small", 24 * PAIRS)
        ptab = sb("ptab", 2 * PAIRS * 9)
        dsk = sb("dsk", GROUPS)
        ones_q = sb("ones_q", P)
        ones_kv = sb("ones_kv", P)
        ada_raw = sb("ada_raw", 48)

        def V(name, k):
            a, _ = VEC[name]
            return vec[:, a + k:a + k + 1]

        def VV(name):
            a, n = VEC[name]
            return vec[:, a:a + n]

        ring = pages(0, RING)
        XN = pages(4, FT)
        XS = pages(12, 4)
        SS = page(12, 4).rearrange("p (i q n) -> p i q n", i=2, q=PAIRS)
        YF = pages(12, 4)
        GS = pages(16, 4)
        WB = page(20, 4).rearrange("p (i q n) -> p i q n", i=2, q=PAIRS)
        CQ = pages(20, 2)
        CKV = page(22)
        KR = page(23)
        GSB = page(24, 4).rearrange("p (g n) -> p g n", g=GROUPS)
        GM = pages(24, 4)
        UU = page(28, 4).rearrange("p (g n) -> p g n", g=GROUPS)
        TMPA = page(28, 2)
        TMPB = page(30, 2)
        PW = page(32, 4).rearrange("p (q i n) -> p q i n", q=PAIRS, i=2)
        TM = page(36, 4).rearrange("p (g n) -> p g n", g=GROUPS)
        CP = cols(40 * PAGE, 40 * PAGE + 2 * PAIRS * 144).rearrange("p (i q n) -> p i q n", i=2, q=PAIRS)
        _e0 = 40 * PAGE + 2 * PAIRS * 144
        EE = cols(_e0, _e0 + 2 * PAIRS * CHUNKS).rearrange("p (i q n) -> p i q n", i=2, q=PAIRS)
        _bc = 48 * PAGE + 512
        BC = cols(_bc, _bc + 4 * 256).rearrange("p (i q c) -> p i q c", i=4, q=PAIRS)
        KB = cols(_bc + 1024, _bc + 1024 + 512).rearrange("p (i q c) -> p i q c", i=2, q=PAIRS)
        QN, QR, KN = pages(28, 4), pages(32, 4), pages(36, 4)
        VT = pages(40, 4).rearrange("p k (a d) -> p (k a) d", a=2)
        KROT, CM = page(44), page(45)
        COS, SIN = page(48), page(49)
        OBUF = [page(12 + i).rearrange("p (k d) -> p k d", k=8) for i in range(2)]
        PP, PT_IN = pages(28, FT), pages(36, 2)
        X2, X2_SUM = pages(42, FT), page(15)

        def sm(x):
            return small[:, x * PAIRS:(x + 1) * PAIRS]

        x_dram = nc.dram_tensor("ssm_in_by_feature", (512, SEQ), F32, kind="Internal").ap()
        y_dram = nc.dram_tensor("ssm_out_by_feature", (512, SEQ), F32, kind="Internal").ap()

        Q2, K2 = pages(12, 8), pages(20, 4)
        V2 = page(24, 4).rearrange("p (k d) -> p k d", k=8)
        OAT = pages(28, 4)
        ONT = [page(12 + 2 * k) for k in range(4)]
        TB = [cols(37 * PAGE, 37 * PAGE + 1920), cols(39 * PAGE, 39 * PAGE + 1920)]
        NB = [cols(37 * PAGE, 37 * PAGE + 1536), cols(37 * PAGE + 1536, 40 * PAGE)]
        COLM = cols(40 * PAGE, 40 * PAGE + 64)
        ROWM = cols(40 * PAGE + 64, 40 * PAGE + 704)
        MRG, GT = pages(20, FT), pages(38, 4)
        ACTV, UPB = pages(12, N_UP), pages(38, 4)
        TEMPS_4 = (page(42), page(43), page(44))
        TEMPS_5 = (page(28), page(29), page(30))
        HV, HV2 = pages(24, FT), pages(20, FT)
        X3, X4 = pages(12, FT), pages(4, FT)
        HH, HL = rounded_pages("h_high", 4, FT), rounded_pages("h_low", 42, FT)
        WR = rounded_pages("w_parts", 34, 4)
        AR = rounded_pages("ffn_parts", 38, 4)
        x_spill = nc.dram_tensor("residual", (D, SEQ), F32, kind="Internal").ap()\
            .rearrange("(k p) t -> p k t", p=P)
        relb, gains, zero = sb("relb", 8), sb("gains", 16), sb("zero", 1)
        dist_dram = nc.dram_tensor("bias_by_distance", (HEADS2, 2048), F32, kind="Internal").ap()
        conv = vec[:, VEC["conv_w"][0]:VEC["conv_w"][0] + 8 * N_UP]

        def pg(view, m):
            return view[:, m, :] if isinstance(m, int) else \
                view[:, bass.ds(m, 1), :].rearrange("p k t -> p (k t)")

        def one(view, m):
            return view[:, m:m + 1] if isinstance(m, int) else view[:, bass.ds(m, 1)]

        block = ctx.enter_context(nc.Block())

        def turned_at(k):
            return slice((k % 2) * BANK + k // 2 * P, (k % 2) * BANK + k // 2 * P + P)

        def odd_copies(items, j):
            return sum(it[2] > P for it in items[:j + 1])

        LAG = 1

        def steps_of(items, per_turn, turns):
            out_, left = [], list(range(len(turns)))
            for i in range(len(items)):
                out_.append(i)
                if left and i == (left[0] + 1) * per_turn + LAG + 2:
                    out_.append(str(left.pop(0)))
            return out_ + [None] * (LAG + 1) + [str(x) for x in left]

        def attention_pe(pe, A, bufs, items, per_turn, turns):
            SBUF, PTB = bufs
            n, step, used = len(items), 0, 0
            for what in steps_of(items, per_turn, turns):
                if what is not None:
                    if used >= 2:
                        pe.wait_ge(S(f"{A}_scores_read"), used - 1)
                    pair = two(2 * (used % 2))
                    used += 1
                if isinstance(what, str):
                    x = int(what)
                    pe.wait_ge(S(f"{A}_out_read"), (x + 1) * per_turn)
                    for k in range(8):
                        mm = pe.transpose(pair[:, k * P:(k + 1) * P], turns[x][0][:, k, :], ident[:])
                    mm.then_inc(S(f"{A}_scores"), 1)
                    continue
                i = step
                step += 1
                if i < n:
                    for c0, c1, lhsT, rhs, st, sp_ in items[i][0]:
                        mm = pe.matmul(pair[:, c0:c1], lhsT, rhs, start=st, stop=sp_)
                    mm.then_inc(S(f"{A}_scores"), 1)
                j = i - LAG
                if 0 <= j < n:
                    w = items[j][2]
                    pe.wait_ge(S(f"{A}_exp"), j + 1)
                    if j >= 1:
                        pe.wait_ge(S(f"{A}_pt_dve"), j)
                        if odd_copies(items, j - 1):
                            pe.wait_ge(S(f"{A}_pt_act"), odd_copies(items, j - 1))
                    for k in range(w // P):
                        mm = pe.transpose(two(4)[:, turned_at(k)],
                                          SBUF[j % NSB][:, k * P:(k + 1) * P], ident[:])
                    mm.then_inc(S(f"{A}_turned"), 1)
                j = i - LAG - 1
                if 0 <= j < n:
                    w, values, d = items[j][2:5]
                    pe.wait_ge(S(f"{A}_pt_dve"), j + 1)
                    if odd_copies(items, j):
                        pe.wait_ge(S(f"{A}_pt_act"), odd_copies(items, j))
                    if j >= 2:
                        pe.wait_ge(S(f"{A}_out_read"), j - 1)
                    for k in range(w // P):
                        mm = pe.matmul(ps[:, 6 + j % 2, 0:d], PTB[j % 2][:, turned_at(k)], values(k),
                                       start=k == 0, stop=k == w // P - 1)
                    mm.then_inc(S(f"{A}_out"), 1)

        def attention_dve(dve, A, bufs, items, per_turn, turns, scale, before):
            SBUF, PTB = bufs
            n, step, used = len(items), 0, 0
            for what in steps_of(items, per_turn, turns):
                if what is not None:
                    pair = two(2 * (used % 2))
                    used += 1
                if isinstance(what, str):
                    _, dst, times = turns[int(what)]
                    dve.wait_ge(S(f"{A}_scores"), used)
                    if times is None:
                        dve.tensor_copy(dst, pair).then_inc(S(f"{A}_scores_read"), 1)
                    else:
                        dve.tensor_tensor(dst, pair, times, ALU.mult).then_inc(S(f"{A}_scores_read"), 1)
                    continue
                i = step
                step += 1
                if i < n:
                    bias, w = items[i][1:3]
                    before(i)
                    dve.wait_ge(S(f"{A}_scores"), used)
                    if i >= NSB:
                        dve.wait_ge(S(f"{A}_turned"), i - NSB + 1)
                    dve.tensor_tensor_reduce(SBUF[i % NSB][:, 0:w], pair[:, 0:w], bias, 1.0,
                                             -3e38, ALU.add, ALU.max, stat[:, i % 4:i % 4 + 1])\
                        .then_inc(S(f"{A}_scores_read"), 1)
                    dve.wait_ge(S(f"{A}_scores_read"), used)
                    dve.tensor_scalar(stat[:, 4 + i % 4:5 + i % 4], stat[:, i % 4:i % 4 + 1], -scale, None,
                                      ALU.mult).then_inc(S(f"{A}_negmax"), 1)
                j = i - LAG
                if 0 <= j < n:
                    h = (items[j][2] // P + 1) // 2 * P
                    dve.wait_ge(S(f"{A}_exp"), j + 1)
                    dve.reciprocal(stat[:, 12 + j % 4:13 + j % 4], stat[:, 8 + j % 4:9 + j % 4])\
                        .then_inc(S(f"{A}_recip"), 1)
                    dve.wait_ge(S(f"{A}_turned"), j + 1)
                    if j >= 2:
                        dve.wait_ge(S(f"{A}_out"), j - 1)
                    dve.tensor_copy(PTB[j % 2][:, 0:h], two(4)[:, 0:h]).then_inc(S(f"{A}_pt_dve"), 1)
                j = i - LAG - 1
                if 0 <= j < n:
                    d, o = items[j][4:6]
                    dve.wait_ge(S(f"{A}_out"), j + 1)
                    dve.wait_ge(S(f"{A}_recip"), j + 1)
                    dve.tensor_scalar(o, ps[:, 6 + j % 2, 0:d], stat[:, 12 + j % 4:13 + j % 4], None,
                                      ALU.mult).then_inc(S(f"{A}_out_read"), 1)

        def attention_act(act, A, bufs, items, scale):
            SBUF, PTB = bufs
            n = len(items)
            for i in range(n + LAG):
                if i < n:
                    w = items[i][2]
                    act.wait_ge(S(f"{A}_negmax"), i + 1)
                    if i >= 4:
                        act.wait_ge(S(f"{A}_recip"), i - 3)
                    act.activation(SBUF[i % NSB][:, 0:w], SBUF[i % NSB][:, 0:w], ACT.Exp,
                                   bias=stat[:, 4 + i % 4:5 + i % 4], scale=scale,
                                   accum_out=stat[:, 8 + i % 4:9 + i % 4]).then_inc(S(f"{A}_exp"), 1)
                j = i - LAG
                if 0 <= j < n:
                    w = items[j][2]
                    if w > P:
                        h = w // P // 2 * P
                        act.wait_ge(S(f"{A}_turned"), j + 1)
                        if j >= 2:
                            act.wait_ge(S(f"{A}_out"), j - 1)
                        act.activation(PTB[j % 2][:, BANK:BANK + h], two(4)[:, BANK:BANK + h], ACT.Copy)\
                            .then_inc(S(f"{A}_pt_act"), 1)

        def scores_used(items, per_turn, turns, i):
            return [w for w in steps_of(items, per_turn, turns) if w is not None].index(i) + 1

        NSB = 3
        BUFS_1 = ([page(20), page(21), page(22)], [page(47), page(23)])
        BUFS_2 = ([page(32), page(33), page(34)], [page(35), page(36)])

        def mla_items():
            items = []
            for h in range(MLA_HEADS):
                for qb in range(8):
                    w = (qb + 1) * P
                    q = slice(qb * P, (qb + 1) * P)
                    sc = []
                    for c0 in range(0, w, BANK):
                        c1 = min(w, c0 + BANK)
                        sc.append((c0, c1, QN[:, h, q], KN[:, h, c0:c1], True, False))
                        sc.append((c0, c1, QR[:, h, q], KROT[:, c0:c1], False, True))
                    items.append((sc, CM[:, SEQ - w:SEQ], w,
                                  lambda k, h=h: VT[:, k, h * P:(h + 1) * P], P,
                                  OBUF[h % 2][:, qb, :]))
            turns = [(OBUF[h % 2], GM[:, h, :], GM[:, h, :]) for h in range(MLA_HEADS)]
            return items, 8, turns

        def out_pages(second_out):
            return [p_.rearrange("p (k d) -> p k d", k=8) for p_ in (page(41), second_out)]

        def dil_items():
            obuf = out_pages(page(12))
            items = []
            for h in range(HEADS2):
                for qb in range(8):
                    sc = [(c, c + BANK, Q2[:, h, qb * P:(qb + 1) * P], K2[:, h // 2, c:c + BANK], True, True)
                          for c in (0, BANK)]
                    items.append((sc, TB[h % 2][:, P * qb:P * qb + SEQ][:, ::-1], SEQ,
                                  lambda k, h=h: V2[:, k, h * HD:(h + 1) * HD], HD,
                                  obuf[h // 2 % 2][:, qb, (h % 2) * HD:(h % 2) * HD + HD]))
            return items, 16, [(obuf[x % 2], OAT[:, x, :], None) for x in range(4)]

        def na_items():
            obuf = out_pages(page(13))
            items = []
            for h in range(HEADS2):
                for qb in range(8):
                    row0 = min(max(2 * qb - 4, 0), 8)
                    inner = 2 <= qb <= 5
                    w = 640 if inner else BANK
                    k0 = row0 * 64
                    sc = [(c, min(c + BANK, w), Q2[:, h, qb * P:(qb + 1) * P],
                           K2[:, h // 2, k0 + c:k0 + min(c + BANK, w)], True, True) for c in range(0, w, BANK)]
                    a = 2 * qb * 64 - k0
                    bias = NB[h % 2][:, 896:1536][:, ::-1] if inner else NB[h % 2][:, a:a + BANK][:, ::-1]
                    items.append((sc, bias, w,
                                  lambda k, h=h, k0=k0: V2[:, k0 // P + k, h * HD:(h + 1) * HD], HD,
                                  obuf[h // 2 % 2][:, qb, (h % 2) * HD:(h % 2) * HD + HD]))
            return items, 16, [(obuf[x % 2], ONT[x], None) for x in range(4)]

        NORMS = {"ln_emb": 8, "kv_norm": 1, "q_norm": 2, "ln_1": 8, "rms_mix": 8, "rms_ffn": 8, "final": 8}

        def tiles_to(N, k):
            names = list(NORMS)
            return sum(NORMS[x] for x in names[:names.index(N)]) + k

        def norms_to(N):
            return list(NORMS).index(N) + 1

        def centred_to(N, k):
            return (FT if N == "ln_1" else 0) + k

        def norm_pe(pe, N, kts, src, ones_, centered, T, ready=None, parts=FT):
            if centered:
                for k in range(parts):
                    ready(k)
                    for nt in range(2):
                        mm = pe.matmul(ps[:, nt, :], ones_, src(k)[:, nt * BANK:(nt + 1) * BANK],
                                       start=k == 0, stop=k == parts - 1)
                mm.then_inc(S("norm_mean"), 1)
            for k in range(kts):
                pe.wait_ge(S("norm_square"), tiles_to(N, k + 1))
                for nt in range(2):
                    mm = pe.matmul(ps[:, 2 + nt, :], ones_, T[k % 2][:, nt * BANK:(nt + 1) * BANK],
                                   start=k == 0, stop=k == kts - 1)
                mm.then_inc(S("norm_square_used"), 1)

        SUMMED = ("rms_ffn", "final")

        def added_to(N, k):
            return (FT - 1) * (1 + SUMMED.index(N)) + max(k, 1)

        def square_act(act, N, k, src, T):
            if k >= 2:
                act.wait_ge(S("tile_added"), added_to(N, k - 2))
            act.activation(T[k % 2], src(k), ACT.Square).then_inc(S("norm_square"), 1)

        def square_dve(dve, N, k, T):
            if k == 0:
                return
            dve.wait_ge(S("norm_square"), tiles_to(N, k + 1))
            if k >= 2:
                dve.wait_ge(S("tile_added"), added_to(N, k - 1))
            dve.tensor_tensor(T[2], T[0] if k == 1 else T[2], T[k % 2], ALU.add).then_inc(S("tile_added"), 1)

        def sum_pe(pe, N, T):
            pe.wait_ge(S("tile_added"), added_to(N, FT - 1))
            for nt in range(2):
                mm = pe.matmul(ps[:, 2 + nt, :], ones[:], T[2][:, nt * BANK:(nt + 1) * BANK],
                               start=True, stop=True)
            mm.then_inc(S("norm_square_used"), 1)

        def norm_act(act, N, kts, src, dst, gain, bias, epscol, centered, T, then=None):
            if N in SUMMED:
                act.wait_ge(S("norm_square_used"), tiles_to(SUMMED[0], SUMMED.index(N) + 1))
            else:
                for k in range(kts):
                    if centered:
                        act.wait_ge(S("norm_centred"), centred_to(N, k + 1))
                    if k >= 2:
                        act.wait_ge(S("norm_square_used"), tiles_to(N, k - 1))
                    act.activation(T[k % 2], src(k), ACT.Square).then_inc(S("norm_square"), 1)
                act.wait_ge(S("norm_square_used"), tiles_to(N, kts))
            act.activation(T[2], two(2), ACT.Sqrt, bias=eps[:, epscol:epscol + 1]).then_inc(S("norm_std"), 1)
            for k in range(kts):
                act.wait_ge(S("norm_scaled"), tiles_to(N, k + 1))
                if then and k > 0:
                    then(k - 1)
                if bias is None:
                    act.activation(dst(k), dst(k), ACT.Copy, scale=gain(k)).then_inc(S("norm_ready"), 1)
                else:
                    act.activation(dst(k), dst(k), ACT.Identity, scale=gain(k), bias=bias(k))\
                        .then_inc(S("norm_ready"), 1)
            if then:
                then(kts - 1)

        def norm_dve(dve, N, kts, src, dst, centered, T):
            if centered:
                dve.wait_ge(S("norm_mean"), centred_to(N, FT) // FT)
                for k in range(kts):
                    dve.tensor_tensor(src(k), src(k), two(0), ALU.subtract).then_inc(S("norm_centred"), 1)
            dve.wait_ge(S("norm_std"), norms_to(N))
            dve.reciprocal(T[2], T[2]).then_inc(S("norm_rstd"), 1)
            dve.wait_ge(S("norm_rstd"), norms_to(N))
            for k in range(kts):
                dve.tensor_tensor(dst(k), src(k), T[2], ALU.mult).then_inc(S("norm_scaled"), 1)


        TEMPS_1 = (page(24), page(25), page(26))
        TEMPS_2 = (page(44), page(45), page(46))
        TEMPS_3 = (page(12), page(13), page(14))

        BLOCKS_WIN = 32
        B_UKV, B_UQ, B_GLU, B_PP = 32, 33, 35, 37
        B_WOUT = 39
        B_WPG = B_WOUT + 16
        B_QK1 = B_WPG + 16
        B_V1 = B_QK1 + 16
        B_QK2 = B_V1 + 4
        B_V2 = B_QK2 + 16
        B_MERGE = B_V2 + 4
        B_WOUT2 = B_MERGE + 24
        B_UP = B_WOUT2 + 8
        B_DOWN = B_UP + 2 * N_UP
        KINDS = ["split", "raw"] * 8 + ["split"] * 4 + ["split", "raw"] * 8 + ["split"] * 4 + \
            ["split", "split", "raw"] * 8 + ["split"] * (8 + 2 * N_UP + N_UP)
        assert len(KINDS) == B_DOWN + N_UP - B_QK1

        def nth(b):
            return KINDS[:b - B_QK1].count(KINDS[b - B_QK1])

        @block.sync
        def _(sp):
            def load(b, q, src, cols=PAGE):
                sp.dma_start(ring[:, b % RING, 0:cols], src).then_inc(S(f"w_landed{b % RING}"), 16)

            def loads(base, first, srcs):
                for j, (src, cols) in enumerate(srcs):
                    if not (isinstance(first, int) and first + j < RING):
                        sp.wait_ge(S("w_used"), first + (j - RING + 1))
                    load(base + j, None, src, cols)

            def tile_of(w, m):
                return (w[bass.ds(m, 1)].rearrange("a p n -> (a p) n"), w.shape[2])

            def w_in_blocks(i):
                out_ = []
                for j in range(4):
                    out_ += [tile_of(t["w_in"], i * 4 + j), tile_of(t["w_ada"], i * 4 + j)]
                return out_

            loads(0, 0, w_in_blocks(0))
            with sp.Fori(1, 4) as i:
                loads(0, i * 8, w_in_blocks(i))
            loads(B_UKV, B_UKV, [tile_of(t["w_ukv"], 0)])
            loads(B_UQ, B_UQ, [tile_of(t["w_uq"], m) for m in range(2)])
            loads(B_GLU, B_GLU, [tile_of(t["w_glu"], m) for m in range(2)])
            loads(B_PP, B_PP, [tile_of(t["w_pp"], m) for m in range(2)])

            def with_ada(base, w, m0, ada0, its):
                with sp.Fori(0, its) as i:
                    blocks_ = []
                    for j in range(4):
                        blocks_ += [tile_of(w, i * 4 + (m0 + j)), tile_of(t["w_ada"], i * 4 + (ada0 + j))]
                    loads(base, i * 8 + base, blocks_)

            with_ada(B_WOUT, t["w_out"], 0, 16, 2)
            with_ada(B_WPG, t["w_pg"], 0, 24, 2)
            def slot_free(b):
                o = b - RING
                if o < B_QK1:
                    return "w_used", o + 1
                return ("w_split" if KINDS[o - B_QK1] == "split" else "raw_used"), nth(o) + 1

            def stage(b0, per, its, srcs):
                for j, (src, cols) in enumerate(srcs(0)):
                    name, count = slot_free(b0 + j)
                    sp.wait_ge(S(name), count)
                    load(b0 + j, None, src, cols)
                if its > 1:
                    kinds = KINDS[b0 - B_QK1:b0 - B_QK1 + per]
                    more = {"w_split": kinds.count("split"), "raw_used": kinds.count("raw")}
                    with sp.Fori(1, its) as i:
                        for j, (src, cols) in enumerate(srcs(i)):
                            name, count = slot_free(b0 + per + j)
                            sp.wait_ge(S(name), i * more[name] + (count - more[name]))
                            load(b0 + j, None, src, cols)

            def qk_blocks(w, ada0):
                return lambda i: [x for j in range(4) for x in (tile_of(w, i * 4 + j),
                                                                tile_of(t["w_ada"], i * 4 + (ada0 + j)))]

            stage(B_QK1, 8, 2, qk_blocks(t["w_qk_dil"], 32))
            stage(B_V1, 4, 1, lambda i: [tile_of(t["w_v_dil"], b) for b in range(4)])
            stage(B_QK2, 8, 2, qk_blocks(t["w_qk_na"], 40))
            stage(B_V2, 4, 1, lambda i: [tile_of(t["w_v_na"], b) for b in range(4)])
            stage(B_MERGE, 12, 2, lambda i: [x for j in range(4) for x in (
                tile_of(t["w_gates"], i * 8 + 2 * j), tile_of(t["w_gates"], i * 8 + (2 * j + 1)),
                tile_of(t["w_branch"], i * 4 + j))])
            stage(B_WOUT2, 4, 2, lambda i: [tile_of(t["w_out_2"], i * 4 + j) for j in range(4)])
            stage(B_UP, 4, N_UP // 2, lambda i: [tile_of(t["w_up"], i * 4 + j) for j in range(4)])
            stage(B_DOWN, 4, 5, lambda i: [tile_of(t["w_down"], i * 4 + j) for j in range(4)])
            stage(B_DOWN + 20, 2, 1, lambda i: [tile_of(t["w_down"], 20 + j) for j in range(2)])
            for k in range(FT):
                sp.wait_ge(S("norm_ready"), tiles_to("final", k + 1))
                sp.dma_start(out[k * P:(k + 1) * P, :], X4[:, k, :]).then_inc(S("out_written"), 16)
            sp.wait_ge(S("out_written"), 16 * FT)

        @block.gpsimd
        def _(pool):
            pool.memset(TM, 0.0).then_inc(S("tm_zero"), 1)
            pool.wait_ge(S("tm_zero"), 1)
            pool.wait_ge(S("g_skip"), 1)
            for s in range(STEP):
                pool.dma_start(TM[s * GC:(s + 1) * GC, :, s * GC:P], GSB[0:GC, :, 0:P - s * GC])\
                    .then_inc(S("tm_landed"), 16)
            pool.wait_ge(S("tables_built"), 1)
            pool.wait_ge(S("x_in_dram"), 16)
            for s in range(STEP):
                pool.dma_start(UU[s * GC:(s + 1) * GC, :, :],
                               x_dram.rearrange("(g c) t -> c g t", c=GC)[:, :, s * CHUNKS:(s + 1) * CHUNKS])\
                    .then_inc(S("u_landed"), 16)
            pool.wait_ge(S("states_ready"), 1)
            pool.dma_start(page(47).bitcast(I32), t["pos"].partition_broadcast(P)).then_inc(S("pos_landed"), 16)
            pool.wait_ge(S("ssm_ps_read"), 32)
            for s in range(STEP):
                pool.dma_start(y_dram.rearrange("(g c) t -> c g t", c=GC)[:, :, s * CHUNKS:(s + 1) * CHUNKS],
                               UU[s * GC:(s + 1) * GC, :, :]).then_inc(S("y_in_dram"), 16)
            pool.wait_ge(S("y_in_dram"), 16 * STEP)
            pool.dma_start(YF, y_dram.rearrange("(k p) t -> p k t", p=P)).then_inc(S("yf_landed"), 16)
            pool.wait_ge(S("cm_zero"), 1)
            pool.dma_start(CM[:, SEQ - P:SEQ], t["causal"]).then_inc(S("cm_landed"), 16)
            pool.wait_ge(S("norm_ready"), tiles_to("q_norm", 2))
            for half in range(2):
                pool.dma_start(page(46)[64 * half:64 * half + 64, :], KR[0:64, :]).then_inc(S("kr_landed"), 16)
                pool.dma_start(page(47)[64 * half:64 * half + 64, :], KR[64:128, :]).then_inc(S("kr_landed"), 16)
            pool.wait_ge(S("mla_out"), 32)
            pool.dma_start(PT_IN, t["pT"].rearrange("(k p) t -> p k t", p=P)).then_inc(S("p_landed"), 16)
            def split(b, i=0, per=0):
                n, more = nth(b), KINDS[b - B_QK1:b - B_QK1 + per].count("split")
                pool.wait_ge(S(f"w_landed{b % RING}"), i * (16 * per // RING) + 16 * (b // RING + 1))
                if (n >= 2 or per) and b < B_DOWN + 2:
                    pool.wait_ge(S("w_used"), i * more + (B_QK1 + n - 1))
                elif b >= B_DOWN + 2:
                    pool.wait_ge(S("down_used"), 2 * (b - B_DOWN) - 2)
                raw = ring[:, b % RING, :]
                pool.tensor_tensor(WR[n % 2], raw, zero[:, 0:1].to_broadcast((P, PAGE)), ALU.add)\
                    .then_inc(S("w_high"), 1)
                pool.wait_ge(S("w_high"), i * more + (n + 1))
                pool.tensor_tensor(WR[2 + n % 2], raw, WR[n % 2].bitcast(F32),
                                   ALU.subtract).then_inc(S("w_split"), 1)

            def split_stage(b0, per, its):
                kinds = KINDS[b0 - B_QK1:b0 - B_QK1 + per]
                for j in range(per):
                    if kinds[j] == "split":
                        split(b0 + j)
                if its > 1:
                    with pool.Fori(1, its) as i:
                        for j in range(per):
                            if kinds[j] == "split":
                                split(b0 + j, i, per)

            pool.memset(zero[:], 0.0).then_inc(S("relb_ones"), 1)
            pool.memset(relb[0:33, :], 1.0).then_inc(S("relb_ones"), 1)
            pool.wait_ge(S("relb_ones"), 2)
            pool.dma_start(relb[0:32, :], t["rel_bias"]).then_inc(S("relb_landed"), 16)
            pool.wait_ge(S("kr_landed"), 64)
            pool.wait_ge(S("mla_out_read"), 32)
            pool.dma_start(page(20, 2)[0:33, :], t["onehot"]).then_inc(S("onehot_landed"), 16)
            pool.wait_ge(S("norm_scaled"), tiles_to("rms_mix", FT))
            pool.memset(page(12, 8), 0.0).then_inc(S("dil_q_zero"), 1)
            split_stage(B_QK1, 8, 2)
            split_stage(B_V1, 4, 1)
            pool.wait_ge(S("dil_v_tiles"), 8)
            pool.wait_ge(S("dist_in_dram"), 16)
            for h in range(HEADS2):
                if h >= 2:
                    pool.wait_ge(S("dil_scores_read"), scores_used(*dil_items(), 8 * (h - 2) + 7))
                pool.dma_start(TB[h % 2], bass.AP(dist_dram.tensor, h * 2048, [[1, P], [1, 1920]]))\
                    .then_inc(S(f"dist_table{h % 2}"), 16)
            pool.wait_ge(S("dil_scores_read"), 64 + 4)
            pool.wait_ge(S("dil_out_read"), 64)
            pool.memset(page(12)[64:P, :], 0.0).then_inc(S("na_q_zero"), 1)
            pool.wait_ge(S("na_q_zero"), 1)
            split_stage(B_QK2, 8, 2)
            split_stage(B_V2, 4, 1)
            pool.wait_ge(S("na_v_tiles"), 8)
            pool.dma_start(COLM, t["na_masks"][:, 0:64]).then_inc(S("na_masks_landed"), 16)
            pool.dma_start(ROWM, t["na_masks"][:, 64:704]).then_inc(S("na_masks_landed"), 16)
            pool.wait_ge(S("na_masks_landed"), 32)
            for h in range(HEADS2):
                if h >= 2:
                    pool.wait_ge(S("na_scores_read"), scores_used(*na_items(), 8 * (h - 2) + 7))
                for rr in range(2):
                    src = bass.AP(t["rpb"].tensor, (15 * h + rr) * P, [[1, 64], [P, 14], [1, 64]])
                    pool.dma_start(NB[h % 2][64 * rr:64 * rr + 64, 0:896].rearrange("p (e c) -> p e c", c=64),
                                   src).then_inc(S(f"na_bias{h % 2}"), 16)
                pool.wait_ge(S(f"na_bias{h % 2}"), 32 * (h // 2 + 1))
                if h:
                    pool.wait_ge(S("na_table"), 2 * h)
                u = NB[h % 2][:, 0:896].rearrange("p (e c) -> p e c", c=64)
                pool.tensor_tensor(u, u, COLM.unsqueeze(1).to_broadcast((P, 14, 64)), ALU.add)\
                    .then_inc(S("na_table"), 1)
                pool.wait_ge(S("na_table"), 2 * h + 1)
                pool.tensor_tensor(NB[h % 2][:, 896:1536], NB[h % 2][:, 128:768], ROWM, ALU.add)\
                    .then_inc(S("na_table"), 1)
            pool.wait_ge(S("na_scores_read"), 64 + 4)
            pool.wait_ge(S("na_out_read"), 64)
            pool.wait_ge(S("na_table"), 16)
            split_stage(B_MERGE, 12, 2)
            split_stage(B_WOUT2, 4, 2)
            split_stage(B_UP, 4, N_UP // 2)
            for b in range(B_DOWN, B_DOWN + N_UP):
                split(b)

        @block.scalar
        def _(act):
            for h in range(4):
                act.dma_start(XN[:, 2 * h:2 * h + 2, :], t["xT"].rearrange("(k p) t -> p k t", p=P)
                              [:, 2 * h:2 * h + 2, :]).then_inc(S(f"x_landed{h}"), 16)
            act.dma_start(vec[:], t["vec"]).then_inc(S("vec_landed"), 16)
            act.dma_start(ident[:], t["ident"]).then_inc(S("ident_landed"), 16)
            act.dma_start(small[:, 0:3 * PAIRS], t["ssm"][:, 0:3 * PAIRS]).then_inc(S("ssm_landed"), 16)
            act.dma_start(BC, t["ssm"][:, 3 * PAIRS:].rearrange("p (i q c) -> p i q c", i=4, q=PAIRS))\
                .then_inc(S("bc_landed"), 16)
            act.dma_start(dsk[0:GC, :], t["dsk"]).then_inc(S("dsk_landed"), 16)
            act.dma_start(rope_c[:], t["rope_c"]).then_inc(S("rope_c_landed"), 16)
            act.wait_ge(S("vec_landed"), 16)
            act.activation(csilu[:], VV("c"), ACT.Silu).then_inc(S("c_ready"), 1)
            act.wait_ge(S("ssm_landed"), 16)
            act.activation(sm(3), sm(2), ACT.Exp).then_inc(S("dt_ready"), 1)
            act.wait_ge(S("dt_are"), 1)
            act.activation(sm(6), sm(4), ACT.Exp).then_inc(S("mag_ready"), 1)
            act.wait_ge(S("theta_reduced"), 1)
            act.activation(sm(7), sm(5), ACT.Sin).then_inc(S("sin_ready"), 1)
            act.activation(sm(8), sm(5), ACT.Sin, scale=0.5).then_inc(S("sin_ready"), 1)
            act.wait_ge(S("eps_set"), 2)
            norm_act(act, "ln_emb", FT, lambda k: XN[:, k, :], lambda k: XN[:, k, :],
                     lambda k: V("ln_emb_g", k), lambda k: V("ln_emb_b", k), 0, True, TEMPS_1)

            def z(tile, dst, func):
                act.wait_ge(S("z_tile"), tile + 1)
                src = two(2 * (tile % 2))
                if tile < 4:
                    dst = dst.rearrange("p (s n) -> p n s", s=STEP)
                    src = src.rearrange("p (n s) -> p n s", s=STEP)
                act.activation(dst, src, func).then_inc(S("z_free"), 1)

            def ada_read(group, last_block):
                if group < 8:
                    act.wait_ge(S("w_used"), last_block + 1)
                else:
                    act.wait_ge(S("raw_used"), 4 * (group - 7))
                act.activation(ada_raw[:, 4 * group:4 * group + 4], ps[:, 4, 0:4], ACT.Copy)\
                    .then_inc(S("ada_read"), 1)

            for tile in range(4):
                z(tile, XS[:, tile, :], ACT.Copy)
            ada_read(0, 7)
            act.wait_ge(S("z_free"), 4)
            act.dma_start(x_dram.rearrange("(k p) t -> p k t", p=P), XS).then_inc(S("x_in_dram"), 16)
            for tile in range(4, 8):
                z(tile, GS[:, tile - 4, :], ACT.Silu)
            ada_read(1, 15)
            for x in range(8):
                act.wait_ge(S("ssm_ps"), x + 1)
                act.activation(PW[:, 2 * x:2 * x + 2, :, :].rearrange("p q i n -> p (q i n)"),
                               ps[:, 5 + x % 2, :], ACT.Copy).then_inc(S("ssm_ps_read"), 1)
            for x in range(8, 16):
                r, odd = (x - 8) // 2, x % 2
                act.wait_ge(S("ssm_ps"), x + 1)
                act.activation(GSB[0:GC, 8 * r + odd:8 * r + 8:2, :],
                               ps[0:GC, 5 + x % 2, :].rearrange("p (g n) -> p g n", g=4), ACT.Copy)\
                    .then_inc(S("ssm_ps_read"), 1)
            for tile in range(8, 12):
                z(tile, CQ[:, tile - 8, :] if tile < 10 else (CKV if tile == 10 else KR), ACT.Copy)
            ada_read(2, 23)
            act.wait_ge(S("u_landed"), 16 * STEP)
            for x in range(16, 24):
                q4, i = (x - 16) // 2, x % 2
                act.wait_ge(S("ssm_ps"), x + 1)
                act.activation(SS[:, i, 4 * q4:4 * q4 + 4, :].rearrange("p q n -> p (q n)"),
                               ps[:, 5 + x % 2, :], ACT.Copy).then_inc(S("ssm_ps_read"), 1)
            act.wait_ge(S("tm_landed"), 16 * STEP)
            for tile in range(12, 16):
                z(tile, GM[:, tile - 12, :], ACT.Silu)
            ada_read(3, 31)
            act.wait_ge(S("angle_reduced"), 1)
            act.activation(SIN, COS, ACT.Sin).then_inc(S("rope_sin"), 1)
            act.activation(page(47), COS, ACT.Sin, scale=0.5).then_inc(S("rope_sin"), 1)
            for x in range(24, 32):
                r, odd = (x - 24) // 2, x % 2
                act.wait_ge(S("ssm_ps"), x + 1)
                act.activation(UU[:, 8 * r + odd:8 * r + 8:2, :],
                               ps[:, 5 + x % 2, :].rearrange("p (g n) -> p g n", g=4), ACT.Copy)\
                    .then_inc(S("ssm_ps_read"), 1)
            norm_act(act, "kv_norm", 1, lambda k: CKV, lambda k: CKV, lambda k: V("kv_norm_g", 0), None,
                     1, False, TEMPS_2)
            norm_act(act, "q_norm", 2, lambda k: CQ[:, k, :], lambda k: CQ[:, k, :],
                     lambda k: V("q_norm_g", k), None, 1, False, TEMPS_2)
            act.wait_ge(S("yf_landed"), 16)
            for m in range(4):
                act.wait_ge(S("kv_tile"), m + 1)
                act.activation(KN[:, m, :], two(2 * (m % 2)), ACT.Copy).then_inc(S("kv_free"), 1)
            for kt in range(8):
                act.wait_ge(S("kv_tile"), 4 + kt + 1)
                act.activation(VT[:, kt, :], ps[:, kt % 4, :], ACT.Copy).then_inc(S("kv_free"), 1)
            for m in range(4):
                act.wait_ge(S("q_tile"), m + 1)
                act.activation(QN[:, m, :], two(2 * (m % 2)), ACT.Copy).then_inc(S("q_free"), 1)
            for k in range(4):
                act.activation(YF[:, k, :], YF[:, k, :], ACT.Gelu_apprx_tanh).then_inc(S("yg_ready"), 1)
            for m in range(4):
                act.wait_ge(S("glu_tile"), m + 1)
                if m >= 2:
                    act.wait_ge(S("glu_used"), m - 1)
                act.activation(page(20 + m % 2), two(2 * (m % 2)), ACT.Sigmoid, bias=V("b_glu", m))\
                    .then_inc(S("glu_sig"), 1)
            act.wait_ge(S("glu_used"), 4)
            attention_act(act, "mla", BUFS_1, mla_items()[0], MLA_SCALE)
            for m in range(8):
                act.wait_ge(S("pp_tile"), m + 1)
                act.activation(PP[:, m, :], two(2 * (m % 2)), ACT.Copy).then_inc(S("pp_free"), 1)
            ada_read(4, B_WOUT + 7)
            ada_read(5, B_WOUT + 15)
            for m in range(8):
                if m == 4:
                    ada_read(6, B_WPG + 7)
                act.wait_ge(S("pg_tile"), m + 1)
                if m >= 2:
                    act.wait_ge(S("ple_ready"), m - 1)
                act.activation(page(24 + m % 2), two(2 * (m % 2)), ACT.Sigmoid).then_inc(S("pg_free"), 1)
            ada_read(7, B_WPG + 15)
            norm_act(act, "ln_1", FT, lambda k: X2[:, k, :], lambda k: X2[:, k, :],
                     lambda k: V("ln_g", k), lambda k: V("ln_b", k), 0, True, TEMPS_3)
            def high(k, ready, count, src):
                act.wait_ge(S(ready), count)
                act.activation(HH[k], src[:, k, :], ACT.Copy).then_inc(S("h_high"), 1)

            act.wait_ge(S("gains_made"), 1)
            act.wait_ge(S("norm_ready"), tiles_to("ln_1", FT))
            act.dma_start(x_spill, X2).then_inc(S("x2_spilled"), 16)
            norm_act(act, "rms_mix", FT, lambda k: X2[:, k, :], lambda k: HV[:, k, :],
                     lambda k: gains[:, k:k + 1], lambda k: ada[:, k:k + 1], 1, False, TEMPS_3,
                     lambda k: high(k, "norm_ready", tiles_to("rms_mix", k + 1), HV))
            for x in range(4):
                act.wait_ge(S("dist_tile"), x + 1)
                act.activation(page(22, 2)[0:HEADS2, x * BANK:(x + 1) * BANK], ps[0:HEADS2, 4 + x, :],
                               ACT.Copy).then_inc(S("dist_free"), 1)
            act.wait_ge(S("dist_free"), 4)
            act.dma_start(dist_dram, page(22, 2)[0:HEADS2, :]).then_inc(S("dist_in_dram"), 16)

            def qk_tiles(A, group, base):
                act.wait_ge(S(f"{A}_q_zero"), 1)
                for m in range(8):
                    act.wait_ge(S(f"{A}_qk_tile"), m + 1)
                    src = two(2 * (m % 2))
                    if m < 4:
                        for i in range(2):
                            h = slice(64 * i, 64 * i + 64)
                            ins = act.activation(Q2[h, 2 * m + i, :], src[h, :], ACT.Copy, scale=HD ** -0.5)
                        ins.then_inc(S(f"{A}_qk_free"), 1)
                    else:
                        if A == "dil" and m == 6:
                            act.wait_ge(S("dist_in_dram"), 16)
                        act.activation(K2[:, m - 4, :], src, ACT.Copy).then_inc(S(f"{A}_qk_free"), 1)
                    if m % 4 == 3:
                        ada_read(group + m // 4, base + 8 * (m // 4) + 7)

            def v_tiles(A):
                act.wait_ge(S(f"{A}_v_tiles"), 8)
                for k in range(4):
                    act.activation(V2[:, k, :], ps[:, k, :], ACT.Copy).then_inc(S(f"{A}_v_act"), 1)

            qk_tiles("dil", 8, B_QK1)
            v_tiles("dil")
            attention_act(act, "dil", BUFS_2, dil_items()[0], 1.0)
            qk_tiles("na", 10, B_QK2)
            v_tiles("na")
            attention_act(act, "na", BUFS_2, na_items()[0], 1.0)

            def merge_body(i):
                for j in range(4):
                    for half in range(2):
                        act.wait_ge(S("gate_tile"), i * 8 + (2 * j + half + 1))
                        if not (isinstance(i, int) and i == 0 and j < 2):
                            act.wait_ge(S("gate_used"), i * 4 + (j - 1))
                        act.activation(GT[:, 2 * (j % 2) + half, :], two(2 * half), ACT.Sigmoid)\
                            .then_inc(S("gate_free"), 1)
            merge_body(0)
            with act.Fori(1, 2) as i:
                merge_body(i)
            act.wait_ge(S("branch_tile"), 8)
            act.dma_start(X3, x_spill).then_inc(S("x2_back"), 16)
            for k in range(FT):
                high(k, "gate_used", k + 1, MRG)
            act.wait_ge(S("gains_made"), 2)
            for k in range(FT):
                act.wait_ge(S("x3_ready"), k + 1)
                square_act(act, "rms_ffn", k, lambda k: X3[:, k, :], TEMPS_5)
            act.dma_start(x_spill, X3).then_inc(S("x3_spilled"), 16)
            norm_act(act, "rms_ffn", FT, lambda k: X3[:, k, :], lambda k: HV2[:, k, :],
                     lambda k: gains[:, 8 + k:9 + k], lambda k: ada[:, 24 + k:25 + k], 1, False, TEMPS_5,
                     lambda k: high(k, "norm_ready", tiles_to("rms_ffn", k + 1), HV2))

            def up_body(i):
                for j in range(2):
                    for half in range(2):
                        act.wait_ge(S("up_tile"), i * 4 + (2 * j + half + 1))
                        if not (isinstance(i, int) and i == 0):
                            act.wait_ge(S("ffn_ready"), i * 2 + (j - 1))
                        n = i * 2 + j
                        act.activation(UPB[:, 2 * j + half, :], two(4 * j + 2 * half), ACT.Identity,
                                       scale=one(conv, n + (2 + half) * N_UP),
                                       bias=one(conv, n + (6 + half) * N_UP)).then_inc(S("up_centre"), 1)
                    act.wait_ge(S("up_taps"), i * 4 + (2 * j + 2))
                    act.activation(UPB[:, 2 * j + 1, :], UPB[:, 2 * j + 1, :], ACT.Gelu_apprx_tanh)\
                        .then_inc(S("up_gelu"), 1)
            up_body(0)
            with act.Fori(1, N_UP // 2) as i:
                up_body(i)
            act.wait_ge(S("up_tile"), 2 * N_UP)
            act.dma_start(X4, x_spill).then_inc(S("x3_back"), 16)
            act.wait_ge(S("ffn_ready"), N_UP)
            for kk in range(2 * N_UP):
                if N_UP + 3 <= kk < N_UP + 7:
                    act.wait_ge(S("x4_ready"), kk - N_UP - 2)
                    square_act(act, "final", kk - N_UP - 3, lambda k: X4[:, k, :], TEMPS_4)
                if kk >= 2:
                    act.wait_ge(S("down_used"), kk - 1)
                act.activation(AR[kk % 2], ACTV[:, kk % N_UP, :], ACT.Copy).then_inc(S("ffn_high"), 1)
            for k in range(4, FT):
                act.wait_ge(S("x4_ready"), k + 1)
                square_act(act, "final", k, lambda k: X4[:, k, :], TEMPS_4)
            norm_act(act, "final", FT, lambda k: X4[:, k, :], lambda k: X4[:, k, :],
                     lambda k: V("g_final", k), None, 1, False, TEMPS_4)

        @block.vector
        def _(dve):
            chain = [0]

            def link(ins):
                chain[0] += 1
                ins.then_inc(S("dve_chain"), 1)
                dve.wait_ge(S("dve_chain"), chain[0])

            def tt(o, a, b, op):
                link(dve.tensor_tensor(o, a, b, op))

            def reduce_angle(a, n):
                link(dve.tensor_scalar(n, a, 1.0 / _TWO_PI, ROUND, ALU.mult, ALU.add))
                link(dve.tensor_scalar(n, n, ROUND, None, ALU.subtract))
                for part in (TP1, TP2, TP3):
                    link(dve.scalar_tensor_tensor(a, n, -part, a, ALU.mult, ALU.add))
                link(dve.tensor_scalar(a, a, PI_IN, -PI_IN, ALU.min, ALU.max))

            def cmul(ore, oim, are, aim, bre, bim, t1, t2):
                tt(t1, are, bre, ALU.mult)
                tt(t2, aim, bim, ALU.mult)
                tt(t1, t1, t2, ALU.subtract)
                tt(t2, are, bim, ALU.mult)
                tt(oim, aim, bre, ALU.mult)
                tt(oim, oim, t2, ALU.add)
                link(dve.tensor_copy(ore, t1))

            link(dve.memset(ones[:], 1.0 / D))
            link(dve.memset(ones_q[:], 1.0 / 256))
            link(dve.memset(ones_kv[:], 1.0 / 128))
            dve.memset(eps[:, 0:1], LN_EPS).then_inc(S("eps_set"), 1)
            dve.memset(eps[:, 1:2], RMS_EPS).then_inc(S("eps_set"), 1)
            dve.sem_inc(S("ones_set"), 1)
            dve.wait_ge(S("ssm_landed"), 16)
            dve.wait_ge(S("dt_ready"), 1)
            dve.tensor_tensor(sm(4), sm(3), sm(0), ALU.mult).then_inc(S("dt_are"), 1)
            tt(sm(5), sm(3), sm(1), ALU.mult)
            reduce_angle(sm(5), sm(9))
            dve.sem_inc(S("theta_reduced"), 1)
            norm_dve(dve, "ln_emb", FT, lambda k: XN[:, k, :], lambda k: XN[:, k, :], True, TEMPS_1)
            dve.wait_ge(S("sin_ready"), 2)
            dve.wait_ge(S("mag_ready"), 1)
            tt(sm(9), sm(8), sm(8), ALU.mult)
            link(dve.tensor_scalar(sm(8), sm(9), -2.0, 1.0, ALU.mult, ALU.add))
            PT = ptab[:].rearrange("p (i q j) -> p i q j", i=2, q=PAIRS)
            pre, pim = PT[:, 0], PT[:, 1]
            link(dve.memset(pre[:, :, 0], 1.0))
            link(dve.memset(pim[:, :, 0], 0.0))
            tt(pre[:, :, 1], sm(6), sm(8), ALU.mult)
            tt(pim[:, :, 1], sm(6), sm(7), ALU.mult)
            tt(sm(9), sm(0), sm(0), ALU.mult)
            tt(sm(10), sm(1), sm(1), ALU.mult)
            tt(sm(9), sm(9), sm(10), ALU.add)
            link(dve.reciprocal(sm(9), sm(9)))
            link(dve.tensor_scalar(sm(10), pre[:, :, 1], 1.0, None, ALU.subtract))
            tt(sm(11), sm(10), sm(0), ALU.mult)
            tt(sm(12), pim[:, :, 1], sm(1), ALU.mult)
            tt(sm(11), sm(11), sm(12), ALU.add)
            tt(sm(11), sm(11), sm(9), ALU.mult)
            tt(sm(12), pim[:, :, 1], sm(0), ALU.mult)
            tt(sm(13), sm(10), sm(1), ALU.mult)
            tt(sm(12), sm(12), sm(13), ALU.subtract)
            tt(sm(12), sm(12), sm(9), ALU.mult)
            def smalls(a, n):
                return cols(28 * PAGE + a * 512, 28 * PAGE + a * 512 + PAIRS * n)\
                    .rearrange("p (q n) -> p q n", q=PAIRS)
            for m in (1, 2, 4):
                last = slice(m, m + 1)
                cmul(pre[:, :, m + 1:2 * m + 1], pim[:, :, m + 1:2 * m + 1],
                     pre[:, :, 1:m + 1], pim[:, :, 1:m + 1],
                     pre[:, :, last].to_broadcast((P, PAIRS, m)), pim[:, :, last].to_broadcast((P, PAIRS, m)),
                     smalls(0, m), smalls(1, m))
            kre, kim = (sm(x).unsqueeze(2).to_broadcast((P, PAIRS, 8)) for x in (11, 12))
            ckre, ckim = smalls(4, 8), smalls(5, 8)
            cmul(ckre, ckim, pre[:, :, 0:8][:, :, ::-1], pim[:, :, 0:8][:, :, ::-1], kre, kim,
                 smalls(6, 8), smalls(7, 8))
            dve.wait_ge(S("bc_landed"), 16)

            def steps_by_channels(x, n):
                return x.unsqueeze(3).to_broadcast((P, PAIRS, n, GC))

            def channels_by_steps(x, n):
                return x.unsqueeze(2).to_broadcast((P, PAIRS, n, GC))

            def by_step(x, n):
                return x.rearrange("p q (s c) -> p q s c", c=GC)

            W0, W1 = by_step(WB[:, 0], 8), by_step(WB[:, 1], 8)
            ta = page(32, 2).rearrange("p (q s c) -> p q s c", q=PAIRS, c=GC)
            tb = page(34, 2).rearrange("p (q s c) -> p q s c", q=PAIRS, c=GC)
            B0, B1 = channels_by_steps(BC[:, 0], 8), channels_by_steps(BC[:, 1], 8)
            K0, K1 = steps_by_channels(ckre, 8), steps_by_channels(ckim, 8)
            tt(W0, K0, B0, ALU.mult)
            tt(ta, K1, B1, ALU.mult)
            tt(W0, W0, ta, ALU.subtract)
            tt(W1, K0, B1, ALU.mult)
            tt(tb, K1, B0, ALU.mult)
            tt(W1, W1, tb, ALU.add)
            dve.sem_inc(S("w_table"), 1)
            kre, kim = (sm(x).unsqueeze(2).to_broadcast((P, PAIRS, GC)) for x in (11, 12))
            cmul(KB[:, 0], KB[:, 1], BC[:, 0], BC[:, 1], kre, kim, smalls(6, 16), smalls(7, 16))
            C0, C1 = channels_by_steps(BC[:, 2], 9), channels_by_steps(BC[:, 3], 9)
            A0, A1 = steps_by_channels(pre, 9), steps_by_channels(pim, 9)
            Q0, Q1 = by_step(CP[:, 0], 9), by_step(CP[:, 1], 9)
            tc = cols(28 * PAGE, 28 * PAGE + PAIRS * 144).rearrange("p (q s c) -> p q s c", q=PAIRS, c=GC)
            tt(Q0, A0, C0, ALU.mult)
            tt(tc, A1, C1, ALU.mult)
            tt(Q0, Q0, tc, ALU.subtract)
            tt(Q1, A0, C1, ALU.mult)
            tt(tc, A1, C0, ALU.mult)
            tt(Q1, Q1, tc, ALU.add)
            link(dve.tensor_scalar(Q1, Q1, -1.0, None, ALU.mult))
            dve.sem_inc(S("cp_table"), 1)
            for x in range(3):
                tt(sm(6), sm(6), sm(6), ALU.mult)
                cmul(sm(8), sm(7), sm(8), sm(7), sm(8), sm(7), sm(9), sm(10))
            link(dve.memset(EE[:, 0, :, 0], 1.0))
            link(dve.memset(EE[:, 1, :, 0], 0.0))
            m = 1
            while m < CHUNKS:
                t1 = page(28, 1).rearrange("p (q n) -> p q n", q=PAIRS)[:, :, 0:m]
                t2 = page(29, 1).rearrange("p (q n) -> p q n", q=PAIRS)[:, :, 0:m]
                cmul(EE[:, 0, :, m:2 * m], EE[:, 1, :, m:2 * m], EE[:, 0, :, 0:m], EE[:, 1, :, 0:m],
                     sm(8).unsqueeze(2).to_broadcast((P, PAIRS, m)),
                     sm(7).unsqueeze(2).to_broadcast((P, PAIRS, m)), t1, t2)
                cmul(sm(8), sm(7), sm(8), sm(7), sm(8), sm(7), sm(9), sm(10))
                m *= 2
            dve.sem_inc(S("tables_built"), 1)
            dve.wait_ge(S("ssm_ps_read"), 16)
            dve.wait_ge(S("dsk_landed"), 16)
            dve.wait_ge(S("ident_landed"), 16)
            dg = cols(_bc, _bc + GROUPS * GC, GC).rearrange("p (g c) -> p g c", g=GROUPS)
            tt(dg, ident[0:GC, 0:GC].unsqueeze(1).to_broadcast((GC, GROUPS, GC)),
               dsk[0:GC, :].unsqueeze(2).to_broadcast((GC, GROUPS, GC)), ALU.mult)
            tt(GSB[0:GC, :, 0:GC], GSB[0:GC, :, 0:GC], dg, ALU.add)
            dve.sem_inc(S("g_skip"), 1)
            T1 = page(32, 2).rearrange("p (q n) -> p q n", q=PAIRS)
            T2 = page(34, 2).rearrange("p (q n) -> p q n", q=PAIRS)
            dve.wait_ge(S("ssm_ps_read"), 24)
            E0, E1, S0, S1 = EE[:, 0], EE[:, 1], SS[:, 0], SS[:, 1]
            tt(T1, S0, E1, ALU.mult)
            tt(T2, S1, E1, ALU.mult)
            tt(S0, S0, E0, ALU.mult)
            tt(S0, S0, T2, ALU.add)
            tt(T2, S1, E0, ALU.mult)
            tt(T2, T2, T1, ALU.subtract)
            for q in range(PAIRS):
                decay = sm(6)[:, q:q + 1].to_broadcast((P, CHUNKS))
                dve.tensor_tensor_scan(T1[:, q, :], decay, S0[:, q, :], 0.0, ALU.mult, ALU.add)\
                    .then_inc(S("scanned"), 1)
                dve.tensor_tensor_scan(S1[:, q, :], decay, T2[:, q, :], 0.0, ALU.mult, ALU.add)\
                    .then_inc(S("scanned"), 1)
            dve.wait_ge(S("scanned"), 2 * PAIRS)
            n1 = slice(0, CHUNKS - 1)
            tt(T2[:, :, n1], T1[:, :, n1], E0[:, :, n1], ALU.mult)
            tt(T1[:, :, n1], T1[:, :, n1], E1[:, :, n1], ALU.mult)
            tt(S0[:, :, 1:], S1[:, :, n1], E1[:, :, n1], ALU.mult)
            tt(S0[:, :, 1:], T2[:, :, n1], S0[:, :, 1:], ALU.subtract)
            tt(T2[:, :, n1], S1[:, :, n1], E0[:, :, n1], ALU.mult)
            tt(S1[:, :, 1:], T2[:, :, n1], T1[:, :, n1], ALU.add)
            link(dve.memset(S0[:, :, 0:1], 0.0))
            link(dve.memset(S1[:, :, 0:1], 0.0))
            dve.sem_inc(S("states_ready"), 1)
            pos_i = page(47).bitcast(I32)
            dve.wait_ge(S("pos_landed"), 16)
            link(dve.tensor_copy(COS, pos_i))
            dve.wait_ge(S("rope_c_landed"), 16)
            link(dve.tensor_scalar(COS, COS, rope_c[:, 0:1], None, ALU.mult))
            reduce_angle(COS, SIN)
            dve.sem_inc(S("angle_reduced"), 1)
            dve.wait_ge(S("rope_sin"), 2)
            link(dve.tensor_scalar(SIN, SIN, rope_c[:, 1:2], None, ALU.mult))
            tt(COS, page(47), page(47), ALU.mult)
            link(dve.tensor_scalar(COS, COS, -2.0, 1.0, ALU.mult, ALU.add))
            norm_dve(dve, "kv_norm", 1, lambda k: CKV, lambda k: CKV, False, TEMPS_2)
            norm_dve(dve, "q_norm", 2, lambda k: CQ[:, k, :], lambda k: CQ[:, k, :], False, TEMPS_2)
            dve.wait_ge(S("norm_ready"), tiles_to("q_norm", 2))
            link(dve.memset(CM, 0.0))
            dve.sem_inc(S("cm_zero"), 1)
            link(dve.memset(QR, 0.0))
            dve.wait_ge(S("kr_landed"), 64)
            tt(KROT, page(46), COS, ALU.mult)
            tt(page(46), page(47), SIN, ALU.mult)
            tt(KROT, KROT, page(46), ALU.add)
            for m in range(2):
                dve.wait_ge(S("qr_tile"), m + 1)
                for i in range(2):
                    h = slice(64 * i, 64 * i + 64)
                    tt(QR[h, 2 * m + i, :], two(0)[h, :], COS[h, :], ALU.mult)
                tt(page(46), two(2), SIN, ALU.mult)
                dve.sem_inc(S("qr_free"), 1)
                for i in range(2):
                    h = slice(64 * i, 64 * i + 64)
                    tt(QR[h, 2 * m + i, :], QR[h, 2 * m + i, :], page(46)[h, :], ALU.add)
            dve.sem_inc(S("rotary_ready"), 1)
            for m in range(4):
                dve.wait_ge(S("glu_sig"), m + 1)
                tt(page(20 + m % 2), page(20 + m % 2), YF[:, m, :], ALU.mult)
                link(dve.tensor_tensor(GS[:, m, :].rearrange("p (n s) -> p s n", s=STEP),
                                       GS[:, m, :].rearrange("p (n s) -> p s n", s=STEP),
                                       page(20 + m % 2).rearrange("p (s n) -> p s n", s=STEP), ALU.mult))
                dve.sem_inc(S("glu_used"), 1)
            dve.wait_ge(S("cm_landed"), 16)
            attention_dve(dve, "mla", BUFS_1, *mla_items(), MLA_SCALE, lambda i: None)
            for i in range(2):
                for j in range(4):
                    m = 4 * i + j
                    dve.wait_ge(S("wo_tile"), m + 1)
                    dve.scalar_tensor_tensor(XN[:, m, :], XN[:, m, :], ALPHA, two(2 * (m % 2)),
                                             ALU.mult, ALU.add).then_inc(S("u_ready"), 1)
            for i in range(2):
                for j in range(4):
                    m = 4 * i + j
                    dve.wait_ge(S("pg_free"), m + 1)
                    tt(page(24 + m % 2), page(24 + m % 2), PP[:, m, :], ALU.mult)
                    dve.tensor_tensor(X2[:, m, :], XN[:, m, :], page(24 + m % 2), ALU.add)\
                        .then_inc(S("ple_ready"), 1)
                    dve.wait_ge(S("ple_ready"), m + 1)
                    if m:
                        if m > 1:
                            dve.wait_ge(S("tile_added"), m - 1)
                        dve.tensor_tensor(X2_SUM, X2_SUM if m > 1 else X2[:, 0, :], X2[:, m, :], ALU.add)\
                            .then_inc(S("tile_added"), 1)
            norm_dve(dve, "ln_1", FT, lambda k: X2[:, k, :], lambda k: X2[:, k, :], True, TEMPS_3)
            dve.wait_ge(S("ada_read"), 8)
            tt(ada[:, 0:32], ada_raw[:, 0:32], VV("b_ada")[:, 0:32], ALU.add)
            link(dve.scalar_tensor_tensor(gains[:, 0:8], ada[:, 8:16], 1.0, VV("g_mix"), ALU.add, ALU.mult))
            dve.sem_inc(S("gains_made"), 1)
            norm_dve(dve, "rms_mix", FT, lambda k: X2[:, k, :], lambda k: HV[:, k, :], False, TEMPS_3)

            def low(base, src):
                for k in range(FT):
                    dve.wait_ge(S("h_high"), base + k + 1)
                    dve.tensor_tensor(HL[k], src(k), HH[k].bitcast(F32), ALU.subtract)\
                        .then_inc(S("h_split"), 1)

            dve.wait_ge(S("x2_spilled"), 16)
            dve.wait_ge(S("norm_scaled"), tiles_to("rms_mix", FT))
            low(0, lambda k: HV[:, k, :])

            def v_tiles(A):
                dve.wait_ge(S(f"{A}_v_tiles"), 8)
                for k in range(4, 8):
                    dve.tensor_copy(V2[:, k, :], ps[:, k, :]).then_inc(S(f"{A}_v_dve"), 1)

            def dil_table(i):
                if i % 8 == 0:
                    dve.wait_ge(S(f"dist_table{i // 8 % 2}"), 16 * (i // 16 + 1))

            def na_table(i):
                if i % 8 == 0:
                    dve.wait_ge(S("na_table"), 2 * (i // 8) + 2)
            v_tiles("dil")
            attention_dve(dve, "dil", BUFS_2, *dil_items(), 1.0, dil_table)
            v_tiles("na")
            attention_dve(dve, "na", BUFS_2, *na_items(), 1.0, na_table)
            dve.wait_ge(S("ada_read"), 12)
            tt(ada[:, 32:48], ada_raw[:, 32:48], VV("b_ada")[:, 32:48], ALU.add)
            link(dve.scalar_tensor_tensor(gains[:, 8:16], ada[:, 32:40], 1.0, VV("g_ffn"), ALU.add, ALU.mult))
            dve.sem_inc(S("gains_made"), 1)

            def merge_body(i):
                for j in range(4):
                    a, b = GT[:, 2 * (j % 2), :], GT[:, 2 * (j % 2) + 1, :]
                    dve.wait_ge(S("gate_free"), i * 8 + (2 * j + 2))
                    dve.wait_ge(S("branch_tile"), i * 4 + (j + 1))
                    dve.tensor_tensor(a, a, two(4), ALU.mult).then_inc(S("branch_read"), 1)
                    dve.tensor_tensor(b, b, two(6), ALU.mult).then_inc(S("branch_read"), 1)
                    dve.wait_ge(S("branch_read"), i * 8 + (2 * j + 2))
                    dve.tensor_tensor(pg(MRG, i * 4 + j), a, b, ALU.add).then_inc(S("gate_used"), 1)
            with dve.Fori(0, 2) as i:
                merge_body(i)
            dve.wait_ge(S("gate_used"), 8)
            low(FT, lambda k: MRG[:, k, :])
            dve.wait_ge(S("x2_back"), 16)
            for m in range(FT):
                dve.wait_ge(S("wo2_tile"), m + 1)
                dve.scalar_tensor_tensor(X3[:, m, :], two(2 * (m % 2)), ada[:, 16 + m:17 + m], X3[:, m, :],
                                         ALU.mult, ALU.add).then_inc(S("x3_ready"), 1)
                square_dve(dve, "rms_ffn", m, TEMPS_5)
            dve.wait_ge(S("x3_ready"), 8)
            norm_dve(dve, "rms_ffn", FT, lambda k: X3[:, k, :], lambda k: HV2[:, k, :], False, TEMPS_5)
            low(2 * FT, lambda k: HV2[:, k, :])
            dve.wait_ge(S("x3_spilled"), 16)
            with dve.Fori(0, N_UP // 2) as i:
                for j in range(2):
                    n = i * 2 + j
                    for half in range(2):
                        y, src = UPB[:, 2 * j + half, :], two(4 * j + 2 * half)
                        dve.wait_ge(S("up_centre"), i * 4 + (2 * j + half + 1))
                        dve.scalar_tensor_tensor(y[:, 1:], src[:, :SEQ - 1],
                                                 one(conv, n + (half * N_UP)), y[:, 1:],
                                                 ALU.mult, ALU.add).then_inc(S("up_left"), 1)
                        dve.wait_ge(S("up_left"), i * 4 + (2 * j + half + 1))
                        dve.scalar_tensor_tensor(y[:, :SEQ - 1], src[:, 1:],
                                                 one(conv, n + ((4 + half) * N_UP)), y[:, :SEQ - 1],
                                                 ALU.mult, ALU.add).then_inc(S("up_taps"), 1)
                    dve.wait_ge(S("up_gelu"), i * 2 + (j + 1))
                    dve.tensor_tensor(pg(ACTV, n), UPB[:, 2 * j, :], UPB[:, 2 * j + 1, :], ALU.mult)\
                        .then_inc(S("ffn_ready"), 1)
            dve.wait_ge(S("ffn_ready"), N_UP)
            for kk in range(2 * N_UP + 1):
                if kk in (N_UP + 1, 2 * N_UP):
                    g = kk // N_UP - 1
                    dve.wait_ge(S("down_used"), N_UP * (g + 1))
                    dve.wait_ge(S("x3_back"), 16)
                    for j in range(4):
                        x = X4[:, 4 * g + j, :]
                        dve.scalar_tensor_tensor(x, two(2 * j), ada[:, 40 + 4 * g + j:41 + 4 * g + j], x,
                                                 ALU.mult, ALU.add).then_inc(S("x4_ready"), 1)
                if N_UP + 4 <= kk < N_UP + 8:
                    square_dve(dve, "final", kk - N_UP - 4, TEMPS_4)
                if kk < 2 * N_UP:
                    dve.wait_ge(S("ffn_high"), kk + 1)
                    dve.tensor_tensor(AR[2 + kk % 2], ACTV[:, kk % N_UP, :],
                                      AR[kk % 2].bitcast(F32), ALU.subtract).then_inc(S("ffn_split"), 1)
            for k in range(4, FT):
                square_dve(dve, "final", k, TEMPS_4)
            norm_dve(dve, "final", FT, lambda k: X4[:, k, :], lambda k: X4[:, k, :], False, TEMPS_4)

        @block.tensor
        def _(pe):
            def block_landed(b, q=None):
                pe.wait_ge(S(f"w_landed{b % RING}"), 16 * (b // RING + 1) if q is None else q * 16 + 16)

            def tile(bank, slot, rhs, kts=FT, at=0, start=True, stop=True, k0=0, step=P, give_back=False, ready=None):
                for k in range(kts):
                    if ready:
                        ready(k)
                    for nt in range(2):
                        mm = pe.matmul(ps[:, bank + nt, :], ring[:, slot, at + k * step:at + k * step + P],
                                       rhs(k0 + k)[:, nt * BANK:(nt + 1) * BANK],
                                       start=start and k == 0, stop=stop and k == kts - 1)
                        if give_back and k == 0 and nt == 0:
                            mm.then_inc(S("w_used"), 1)
                return mm

            def four_with_ada(i, base, group, done, free, rhs, ready=None):
                for j in range(4):
                    b = base + 2 * j
                    block_landed(b, 2 * i + b // RING)
                    if not (isinstance(i, int) and i == 0) or j >= 2:
                        pe.wait_ge(S(free), 4 * i + (j - 1))
                    tile(2 * (j % 2), b % RING, rhs, ready=ready if j == 0 else None).then_inc(S(done), 1)
                    b += 1
                    block_landed(b, 2 * i + b // RING)
                    if j == 0 and not (isinstance(group, int) and group == 0):
                        pe.wait_ge(S("ada_read"), group)
                    for k in range(FT):
                        mm = pe.matmul(ps[:, 4, j:j + 1], ring[:, b % RING, k * P:(k + 1) * P],
                                       csilu[:, k:k + 1], start=k == 0, stop=k == FT - 1)
                        if k in (0, FT - 1):
                            mm.then_inc(S("w_used"), 1)

            pe.wait_ge(S("ones_set"), 1)
            norm_pe(pe, "ln_emb", FT, lambda k: XN[:, k, :], ones[:], True, TEMPS_1,
                    lambda k: pe.wait_ge(S(f"x_landed{k // 2}"), 16))
            pe.wait_ge(S("c_ready"), 1)
            xn = lambda k: XN[:, k, :]
            four_with_ada(0, 0, 0, "z_tile", "z_free", xn,
                          lambda k: pe.wait_ge(S("norm_ready"), tiles_to("ln_emb", k + 1)))
            four_with_ada(1, 0, 1, "z_tile", "z_free", xn)
            pe.wait_ge(S("w_table"), 1)
            pe.wait_ge(S("ident_landed"), 16)
            for x in range(8):
                if x >= 2:
                    pe.wait_ge(S("ssm_ps_read"), x - 1)
                for j in range(4):
                    mm = pe.transpose(ps[:, 5 + x % 2, j * P:(j + 1) * P], WB[:, j % 2, 2 * x + j // 2, :],
                                      ident[:])
                mm.then_inc(S("ssm_ps"), 1)
            pe.wait_ge(S("cp_table"), 1)
            for x in range(8, 16):
                pe.wait_ge(S("ssm_ps_read"), x - 1)
                r, odd = (x - 8) // 2, x % 2
                h = slice(64 * odd, 64 * odd + 64)
                for j in range(4):
                    q = 4 * r + j
                    for i in range(2):
                        mm = pe.matmul(ps[0:GC, 5 + x % 2, j * P:(j + 1) * P], KB[h, i, q, :],
                                       CP[h, i, q, 0:P], start=i == 0, stop=i == 1)
                mm.then_inc(S("ssm_ps"), 1)
            four_with_ada(2, 0, 2, "z_tile", "z_free", xn)
            pe.wait_ge(S("u_landed"), 16 * STEP)
            for x in range(16, 24):
                pe.wait_ge(S("ssm_ps_read"), x - 1)
                q4, i = (x - 16) // 2, x % 2
                for j in range(4):
                    q = 4 * q4 + j
                    for g2 in range(2):
                        mm = pe.matmul(ps[64 * g2:64 * g2 + 64, 5 + x % 2, j * P:(j + 1) * P],
                                       PW[:, q, i, 64 * g2:64 * g2 + 64], UU[:, 2 * q + g2, :],
                                       start=True, stop=True)
                mm.then_inc(S("ssm_ps"), 1)
            four_with_ada(3, 0, 3, "z_tile", "z_free", xn)
            pe.wait_ge(S("states_ready"), 1)
            pe.wait_ge(S("tm_landed"), 16 * STEP)
            for x in range(24, 32):
                pe.wait_ge(S("ssm_ps_read"), x - 1)
                r, odd = (x - 24) // 2, x % 2
                h = slice(64 * odd, 64 * odd + 64)
                for j in range(4):
                    q = 4 * r + j
                    o = ps[:, 5 + x % 2, j * P:(j + 1) * P]
                    pe.matmul(o, TM[:, 2 * q + odd, :], UU[:, 2 * q + odd, :], start=True, stop=False)
                    for i in range(2):
                        mm = pe.matmul(o, CP[h, i, q, GC:GC + P], SS[h, i, q, :], start=False, stop=i == 1)
                mm.then_inc(S("ssm_ps"), 1)
            pe.wait_ge(S("z_free"), 16)
            norm_pe(pe, "kv_norm", 1, None, ones_kv[:], False, TEMPS_2)
            pe.wait_ge(S("norm_std"), norms_to("kv_norm"))
            norm_pe(pe, "q_norm", 2, None, ones_q[:], False, TEMPS_2)
            pe.wait_ge(S("norm_std"), norms_to("q_norm"))
            pe.wait_ge(S("norm_ready"), tiles_to("kv_norm", 1))
            b = B_UKV
            block_landed(B_UKV)
            for m in range(4):
                if m >= 2:
                    pe.wait_ge(S("kv_free"), m - 1)
                tile(2 * (m % 2), b % RING, lambda k: CKV, kts=1, at=m * P).then_inc(S("kv_tile"), 1)
            for kt in range(8):
                if kt == 0:
                    pe.wait_ge(S("kv_free"), 4)
                if kt >= 4:
                    pe.wait_ge(S("kv_free"), kt + 1)
                mm = pe.matmul(ps[:, kt % 4, :], CKV[:, kt * P:(kt + 1) * P], ring[:, b % RING, BANK:2 * BANK],
                               start=True, stop=True).then_inc(S("kv_tile"), 1)
            pe.wait_ge(S("kv_tile"), 12)
            pe.sem_inc(S("w_used"), 1)
            pe.wait_ge(S("norm_ready"), tiles_to("q_norm", 2))
            pe.wait_ge(S("kv_free"), 12)
            block_landed(B_UQ)
            for m in range(4):
                if m >= 2:
                    pe.wait_ge(S("q_free"), m - 1)
                mm = tile(2 * (m % 2), B_UQ % RING, lambda k: CQ[:, k, :], kts=2, at=m * P, step=BANK)
                mm.then_inc(S("q_tile"), 1)
            pe.wait_ge(S("q_tile"), 4)
            pe.sem_inc(S("w_used"), 1)
            block_landed(B_UQ + 1)
            pe.wait_ge(S("q_free"), 4)
            for m in range(2):
                if m == 1:
                    pe.wait_ge(S("qr_free"), 1)
                tile(0, (B_UQ + 1) % RING, lambda k: CQ[:, k, :], kts=2, at=m * P, step=BANK)
                tile(2, (B_UQ + 1) % RING, lambda k: CQ[:, k, :], kts=2, at=(2 + m) * P, step=BANK)\
                    .then_inc(S("qr_tile"), 1)
            pe.wait_ge(S("qr_tile"), 2)
            pe.sem_inc(S("w_used"), 1)
            pe.wait_ge(S("yg_ready"), 4)
            pe.wait_ge(S("qr_free"), 2)
            for m in range(4):
                block_landed(B_GLU + m // 2)
                if m >= 2:
                    pe.wait_ge(S("glu_sig"), m - 1)
                mm = tile(2 * (m % 2), (B_GLU + m // 2) % RING, lambda k: YF[:, k, :], kts=4,
                          at=(m % 2) * P, step=2 * P)
                mm.then_inc(S("glu_tile"), 1)
                if m % 2:
                    pe.wait_ge(S("glu_tile"), m + 1)
                    pe.sem_inc(S("w_used"), 1)
            pe.wait_ge(S("rotary_ready"), 1)
            pe.wait_ge(S("glu_sig"), 4)
            attention_pe(pe, "mla", BUFS_1, *mla_items())
            pe.wait_ge(S("mla_scores_read"), 32 + MLA_HEADS)
            pe.wait_ge(S("p_landed"), 16)
            for m in range(8):
                block_landed(B_PP + m // 4)
                if m >= 2:
                    pe.wait_ge(S("pp_free"), m - 1)
                mm = tile(2 * (m % 2), (B_PP + m // 4) % RING, lambda k: PT_IN[:, k, :], kts=2,
                          at=(m % 4) * P, step=BANK)
                mm.then_inc(S("pp_tile"), 1)
                if m % 4 == 3:
                    pe.wait_ge(S("pp_tile"), m + 1)
                    pe.sem_inc(S("w_used"), 1)
            pe.wait_ge(S("pp_free"), 8)
            mixed = lambda k: GS[:, k, :] if k < 4 else GM[:, k - 4, :]
            four_with_ada(0, B_WOUT, 4, "wo_tile", "u_ready", mixed)
            four_with_ada(1, B_WOUT, 5, "wo_tile", "u_ready", mixed)
            pe.wait_ge(S("u_ready"), 8)
            four_with_ada(0, B_WPG, 6, "pg_tile", "pg_free", xn)
            four_with_ada(1, B_WPG, 7, "pg_tile", "pg_free", xn)
            norm_pe(pe, "ln_1", FT, lambda k: X2_SUM, ones[:], True, TEMPS_3,
                    lambda k: pe.wait_ge(S("tile_added"), FT - 1), 1)
            norm_pe(pe, "rms_mix", FT, None, ones[:], False, TEMPS_3)
            pe.wait_ge(S("relb_landed"), 16)
            pe.wait_ge(S("onehot_landed"), 16)
            for x in range(4):
                pe.matmul(ps[0:HEADS2, 4 + x, :], relb[0:33, :], page(20, 2)[0:33, x * BANK:(x + 1) * BANK],
                          start=True, stop=True).then_inc(S("dist_tile"), 1)
            pe.wait_ge(S("dist_free"), 4)
            pe.wait_ge(S("norm_std"), norms_to("rms_mix"))

            def tile3(bank, slot, give_back=None, waits=None):
                for k in range(FT):
                    if waits is not None:
                        pe.wait_ge(S("h_split"), waits + k + 1)
                    for n, (w_, x_) in enumerate(((0, HH), (0, HL), (2, HH))):
                        for nt in range(2):
                            mm = pe.matmul(ps[:, bank + nt, :], WR[slot + w_][:, k * P:(k + 1) * P],
                                           x_[k][:, nt * BANK:(nt + 1) * BANK],
                                           start=k == 0 and n == 0, stop=k == FT - 1 and n == 2)
                            if give_back and k == 0 and n == 0 and nt == 0:
                                mm.then_inc(S(give_back), 1)
                return mm

            def qk_tiles(A, i, base, group, waits):
                for j in range(4):
                    b = base + 8 * i + 2 * j
                    n = nth(b)
                    pe.wait_ge(S("w_split"), n + 1)
                    if 4 * i + j >= 2:
                        pe.wait_ge(S(f"{A}_qk_free"), 4 * i + j - 1)
                    tile3(2 * (j % 2), n % 2, waits=waits if j == 0 else None)\
                        .then_inc(S(f"{A}_qk_tile"), 1)
                    block_landed(b + 1)
                    if j == 0:
                        pe.wait_ge(S("ada_read"), group)
                    for k in range(FT):
                        mm = pe.matmul(ps[:, 4, j:j + 1], ring[:, (b + 1) % RING, k * P:(k + 1) * P],
                                       csilu[:, k:k + 1], start=k == 0, stop=k == FT - 1)
                        if k in (0, FT - 1):
                            mm.then_inc(S("w_used" if k == 0 else "raw_used"), 1)

            def qkv(A, base_qk, base_v, group):
                qk_tiles(A, 0, base_qk, group, 0 if A == "dil" else None)
                qk_tiles(A, 1, base_qk, group + 1, None)
                pe.wait_ge(S(f"{A}_qk_free"), 8)
                pe.wait_ge(S("ada_read"), group + 2)
                for b in range(4):
                    n = nth(base_v + b)
                    pe.wait_ge(S("w_split"), n + 1)
                    for kt in range(8):
                        for k in range(2):
                            for m, (w_, x_) in enumerate(((0, HH), (0, HL), (2, HH))):
                                mm = pe.matmul(ps[:, kt, :], x_[2 * b + k][:, kt * P:(kt + 1) * P],
                                               WR[n % 2 + w_][:, k * BANK:(k + 1) * BANK],
                                               start=b == 0 and k == 0 and m == 0,
                                               stop=b == 3 and k == 1 and m == 2)
                                if b > 0 and kt == 0 and k == 0 and m == 0:
                                    mm.then_inc(S("w_used"), 1)
                        if b == 3:
                            mm.then_inc(S(f"{A}_v_tiles"), 1)
                pe.wait_ge(S(f"{A}_v_act"), 4)
                pe.wait_ge(S(f"{A}_v_dve"), 4)
                pe.sem_inc(S("w_used"), 1)

            qkv("dil", B_QK1, B_V1, 8)
            attention_pe(pe, "dil", BUFS_2, *dil_items())
            pe.wait_ge(S("dil_scores_read"), 64 + 4)
            pe.wait_ge(S("dil_out_read"), 64)
            qkv("na", B_QK2, B_V2, 10)
            attention_pe(pe, "na", BUFS_2, *na_items())
            pe.wait_ge(S("na_scores_read"), 64 + 4)
            pe.wait_ge(S("na_out_read"), 64)

            def turns_of(b, i, per):
                return i * (per // RING) + b // RING

            def merge_body(i):
                first = isinstance(i, int) and i == 0
                for j in range(4):
                    for half in range(2):
                        n = nth(B_MERGE + 3 * j + half)
                        pe.wait_ge(S("w_split"), i * 8 + (n + 1))
                        if not (first and j == 0):
                            pe.wait_ge(S("gate_free"), i * 8 + (2 * j + half - 1))
                        back = "w_used" if half else None if first and j == 0 else "raw_used"
                        tile3(2 * half, n % 2, back).then_inc(S("gate_tile"), 1)
                    b = B_MERGE + 3 * j + 2
                    block_landed(b, turns_of(b, i, 12))
                    if not (first and j == 0):
                        pe.wait_ge(S("branch_read"), i * 8 + 2 * j)
                    tile(4, b % RING, lambda k: OAT[:, k, :], kts=4, give_back=True)
                    tile(6, b % RING, lambda k: ONT[k], kts=4, at=4 * P).then_inc(S("branch_tile"), 1)
            merge_body(0)
            with pe.Fori(1, 2) as i:
                merge_body(i)
            pe.wait_ge(S("branch_tile"), 8)
            pe.sem_inc(S("raw_used"), 1)
            pe.wait_ge(S("gate_free"), 16)
            pe.wait_ge(S("gate_used"), 8)

            def wo2_body(i):
                first = isinstance(i, int) and i == 0
                for j in range(4):
                    n = nth(B_WOUT2 + j)
                    pe.wait_ge(S("w_split"), i * 4 + (n + 1))
                    if not (first and j < 2):
                        pe.wait_ge(S("x3_ready"), i * 4 + (j - 1))
                    start = first and j == 0
                    tile3(2 * (j % 2), n % 2, None if start else "w_used", FT if start else None)\
                        .then_inc(S("wo2_tile"), 1)
            wo2_body(0)
            with pe.Fori(1, 2) as i:
                wo2_body(i)
            pe.wait_ge(S("wo2_tile"), 8)
            pe.sem_inc(S("w_used"), 1)
            sum_pe(pe, "rms_ffn", TEMPS_5)
            pe.wait_ge(S("norm_std"), norms_to("rms_ffn"))

            def up_body(i):
                first = isinstance(i, int) and i == 0
                for j in range(2):
                    for half in range(2):
                        n = nth(B_UP + 2 * j + half)
                        pe.wait_ge(S("w_split"), i * 4 + (n + 1))
                        if not first:
                            pe.wait_ge(S("up_taps"), i * 4 + (2 * j + half - 3))
                        start = first and j == 0 and half == 0
                        tile3(4 * j + 2 * half, n % 2, None if start else "w_used", 2 * FT if start else None)\
                            .then_inc(S("up_tile"), 1)
            up_body(0)
            with pe.Fori(1, N_UP // 2) as i:
                up_body(i)
            pe.wait_ge(S("up_tile"), 2 * N_UP)
            pe.sem_inc(S("w_used"), 1)
            pe.wait_ge(S("ffn_ready"), N_UP)

            for kk in range(2 * N_UP):
                g, k = divmod(kk, N_UP)
                n = nth(B_DOWN + kk // 2)
                pe.wait_ge(S("w_split"), n + 1)
                pe.wait_ge(S("ffn_split"), kk + 1)
                for m in range(4):
                    if k == 0 and g == 1:
                        pe.wait_ge(S("x4_ready"), m + 1)
                    for q, (w_, x_) in enumerate(((0, 0), (0, 2), (2, 0))):
                        for nt in range(2):
                            at = kk % 2 * BANK + m * P
                            mm = pe.matmul(ps[:, 2 * m + nt, :], WR[n % 2 + w_][:, at:at + P],
                                           AR[kk % 2 + x_][:, nt * BANK:(nt + 1) * BANK],
                                           start=k == 0 and q == 0, stop=k == N_UP - 1 and q == 2)
                mm.then_inc(S("down_used"), 1)
            sum_pe(pe, "final", TEMPS_4)



def kernel(**inputs):
    import numpy as _np
    import concourse.bacc as _bacc
    from concourse import mybir as _mybir
    from concourse.bass_utils import run_bass_kernel_spmd as _run

    g = {k: _np.asarray(v) for k, v in inputs.items()}

    def tiled(w, m=P):
        K, M = w.shape
        return _np.ascontiguousarray(w.reshape(K // P, P, M // m, m).transpose(2, 1, 0, 3)
                                     .reshape(M // m, P, K // P * m))

    def cols(v):
        return v.reshape(-1, P).T

    def halves(w):
        K, M = w.shape
        return w.reshape(K, M // 64, 2, 32)[:, :, ::-1].reshape(K, M)

    w_in = g["w_in"][0]
    xs, gs, cq, ckv, kr, gm = _np.split(w_in, _np.cumsum([512, 512, 256, 128, 64]).tolist(), axis=1)
    uq = g["w_uq"][0].reshape(256, MLA_HEADS, 192)
    uq_plain, uq_rot = uq[:, :, :P].reshape(256, 512), uq[:, :, P:].reshape(256, 256)
    ukv = g["w_ukv"][0].reshape(P, MLA_HEADS, 256)
    ukv = _np.concatenate([ukv[:, :, :P].reshape(P, 512), ukv[:, :, P:].reshape(P, 512)], axis=1)

    def pairs(a):
        a = a.reshape((PAIRS, 2, STATE) + a.shape[2:])
        return _np.moveaxis(a, 0, 2).reshape(P, -1)

    vec = _np.concatenate([cols(g[n].reshape(-1)) for n in (
        "ln_emb_g", "ln_emb_b", "b_glu", "q_norm_g", "kv_norm_g", "ln_g", "ln_b", "c_2", "b_ada_2",
        "g_mix_2", "g_ffn_2", "conv_w_2", "conv_b_2", "g_final_2")], axis=1)
    p_ = _np.arange(P)
    inv_freq = (1.0 / 10000.0 ** (2 * (p_ % 32) / 64.0)).astype(_np.float32)
    sign = _np.where(p_ % 64 < 32, -1.0, 1.0).astype(_np.float32)
    arrays = {
        "xT": g["x"][0].T, "pT": g["p"][0, 0].T, "pos": g["positions"].reshape(SEQ), "vec": vec,
        "ident": _np.eye(P, dtype=_np.float32),
        "causal": _np.where(p_[None, :] > p_[:, None], MASKED, 0.0).astype(_np.float32),
        "rope_c": _np.stack([inv_freq, sign], axis=1),
        "ssm": _np.concatenate([pairs(g["a_re"][0]), pairs(g["a_im"][0]),
                                pairs(_np.repeat(g["log_dt"][0][:, None], STATE, 1)),
                                pairs(g["b_re"][0]), pairs(g["b_im"][0]),
                                pairs(g["c_re"][0].transpose(0, 2, 1)), pairs(g["c_im"][0].transpose(0, 2, 1))],
                               axis=1),
        "dsk": g["d_skip"][0].reshape(GROUPS, GC).T,
        "w_in": tiled(_np.concatenate([xs, gs, cq, ckv, kr, halves(kr), gm], axis=1)),
        "w_ada": tiled(g["w_ada_2"][0]), "w_glu": tiled(g["w_glu"][0], 2 * P),
        "w_uq": tiled(_np.concatenate([uq_plain, uq_rot, halves(uq_rot)], axis=1), 512),
        "w_ukv": tiled(ukv, 1024), "w_pp": tiled(g["w_pp"][0], 512),
        "w_out": tiled(g["w_out"][0]), "w_pg": tiled(g["w_pg"][0]),
    }
    w2 = g["w_in_2"][0]
    dq, dk, dv, nq, nk, nv, ga, gb = _np.split(w2, _np.cumsum([512] * 6 + [1024]).tolist(), axis=1)

    def by_two(w):
        return w.reshape(4, 2, P, 512).transpose(0, 2, 1, 3).reshape(4, P, 1024)

    def alternate(a, b):
        a, b = (w.reshape(w.shape[0], -1, 1, P) for w in (a, b))
        return _np.concatenate([a, b], axis=2).reshape(a.shape[0], -1)

    d = 1023 - _np.arange(2048)
    a = _np.abs(d)
    large = 8 + (_np.log(_np.maximum(a, 1).astype(_np.float32) / 8) / math.log(1024 / 8) * 8).astype(_np.int32)
    bucket = _np.where(d > 0, 16, 0) + _np.where(a < 8, a, _np.minimum(large, 15))
    times = sum(((a % dil == 0) & (a <= win // 2)).astype(int) for win, dil in ((128, 1), (512, 4), (2048, 16)))
    onehot = _np.zeros((33, 2048), _np.float32)
    onehot[bucket, _np.arange(2048)] = 1.0
    onehot[32] = _np.where(times > 0, _np.log(_np.maximum(times, 1)), MASKED)
    cq_, ck_ = p_ % 64, 63 - _np.arange(64)
    start = _np.clip(cq_ - 8, 0, 48)
    colm = _np.where((ck_[None] >= start[:, None]) & (ck_[None] < start[:, None] + 16), 0.0, MASKED)
    dr_ = 5 - _np.arange(10)
    off = dr_[None] - (p_ // 64)[:, None]
    rowm = _np.repeat(_np.where((off >= -4) & (off <= 3), 0.0, MASKED), 64, axis=1)
    rpb = _np.zeros((8, 15, P), _np.float32)
    rpb[:, :, 48:79] = g["na_rpb_2"][0][:, ::-1, ::-1]
    arrays.update({
        "w_qk_dil": tiled(_np.concatenate([dq, dk], axis=1)), "w_v_dil": by_two(dv),
        "w_qk_na": tiled(_np.concatenate([nq, nk], axis=1)), "w_v_na": by_two(nv),
        "w_gates": tiled(alternate(ga, gb)),
        "w_branch": tiled(_np.concatenate([g["w_branch_dil_2"][0], g["w_branch_na_2"][0]], axis=0)),
        "w_out_2": tiled(g["w_out_2"][0]),
        "w_up": tiled(alternate(g["w_up_2"][0][:, :N_UP * P], g["w_up_2"][0][:, N_UP * P:])),
        "w_down": g["w_down_2"][0].reshape(N_UP // 2, 2, P, 2, 512).transpose(3, 0, 2, 1, 4)
                                  .reshape(N_UP, P, 1024),
        "rel_bias": g["rel_bias_2"], "onehot": onehot, "rpb": rpb.reshape(120, P),
        "na_masks": _np.concatenate([colm, rowm], axis=1).astype(_np.float32),
    })
    arrays = {k: _np.ascontiguousarray(v) for k, v in arrays.items()}
    nc = _bacc.Bacc("TRN2", target_bir_lowering=False, num_devices=1)
    t = {n: nc.dram_tensor(n, a.shape, _mybir.dt.from_np(a.dtype), kind="ExternalInput").ap()
         for n, a in arrays.items()}
    out = nc.dram_tensor("out", (D, SEQ), F32, kind="ExternalOutput").ap()
    program(nc, t, out)
    r = _run(nc, [arrays], core_ids=[0])
    return _np.ascontiguousarray(r.results[0]["out"].T)[None]
```
